# Optimizing a Trainium2 kernel written in Bass

```python
import math
import jax
import jax.numpy as jnp
from jax import lax
import numpy as np

D_MODEL = 1024
BATCH = 1
SEQ = 512
DEPTH = 2

CHUNK = 64
Q_BLOCK = 128
D_FF = 4 * D_MODEL
NORM_EPS = 1e-6

FOX_HEADS = 8
FOX_HEAD_DIM = D_MODEL // 16
FOX_W = FOX_HEADS * FOX_HEAD_DIM
FOX_F_BIAS_MEAN = 2.0
GDN_HEADS = 4
GDN_HEAD_DIM = D_MODEL // 8
GDN_W = GDN_HEADS * GDN_HEAD_DIM
GDN_CONV = 4
EVEN_SPLIT = (FOX_W, FOX_W, FOX_W, FOX_HEADS,
              GDN_W, GDN_W, GDN_W, GDN_HEADS, GDN_HEADS, GDN_W)
EVEN_IN = 3 * FOX_W + FOX_HEADS + 4 * GDN_W + 2 * GDN_HEADS

HGRN_EXPAND = 128
HGRN_HEADS = D_MODEL // HGRN_EXPAND
HGRN_HEAD_DIM = HGRN_EXPAND
ODD_IN = 4 * D_MODEL

kernel_name = "fox_gdn_hgrn2_hybrid_trunk"

def rms_norm(x, gain):
    xf = x.astype(jnp.float32)
    y = xf * lax.rsqrt(jnp.mean(xf * xf, axis=-1, keepdims=True) + NORM_EPS)
    return (y * gain.astype(jnp.float32)).astype(x.dtype)

def l2_normalize(x):
    xf = x.astype(jnp.float32)
    return xf * lax.rsqrt(jnp.sum(xf * xf, axis=-1, keepdims=True) + NORM_EPS)

def split_cols(z, sizes):
    out, start = [], 0
    for s in sizes:
        out.append(z[..., start:start + s])
        start += s
    return out

def causal_depthwise_conv(x, w):
    k_w, c = w.shape
    return lax.conv_general_dilated(
        x, w[:, None, :].astype(x.dtype), window_strides=(1,),
        padding=[(k_w - 1, 0)], dimension_numbers=("NWC", "WIO", "NWC"),
        feature_group_count=c)

def squared_relu_mlp(h, w1, w2):
    a = jax.nn.relu(h @ w1)
    return (a * a) @ w2

def forgetting_attention(q, k, v, f_logit):
    b, t, h, dh = q.shape
    c = jnp.cumsum(jax.nn.log_sigmoid(f_logit.astype(jnp.float32)), axis=1)
    c = c.transpose(0, 2, 1)
    scale = dh ** -0.5
    outs = []
    for i in range(t // Q_BLOCK):
        q0, q1 = i * Q_BLOCK, (i + 1) * Q_BLOCK
        s = jnp.einsum("bqhd,bkhd->bhqk", q[:, q0:q1], k[:, :q1]).astype(jnp.float32) * scale
        s = s + c[:, :, q0:q1, None] - c[:, :, None, :q1]
        mask = (q0 + jnp.arange(Q_BLOCK))[:, None] >= jnp.arange(q1)[None, :]
        s = jnp.where(mask, s, -jnp.inf)
        p = jax.nn.softmax(s, axis=-1).astype(v.dtype)
        outs.append(jnp.einsum("bhqk,bkhd->bqhd", p, v[:, :q1]))
    return jnp.concatenate(outs, axis=1)

def gated_delta_rule(q, k, v, log_alpha, beta):
    b, h, t, dk = q.shape
    dv = v.shape[-1]
    n = t // CHUNK
    rs = lambda a: a.reshape(b, h, n, CHUNK, *a.shape[3:])
    q = rs(q * dk ** -0.5)
    k, v = rs(k), rs(v)
    beta = rs(beta)
    g = jnp.cumsum(rs(log_alpha), axis=-1)
    idx = jnp.arange(CHUNK)
    causal = idx[:, None] >= idx[None, :]
    strict = idx[:, None] > idx[None, :]
    decay = jnp.exp(jnp.where(causal, g[..., :, None] - g[..., None, :], -jnp.inf))
    k_beta = k * beta[..., None]
    a_mat = jnp.where(strict, jnp.einsum("bhnck,bhndk->bhncd", k_beta, k) * decay, 0.0)
    eye = jnp.eye(CHUNK, dtype=jnp.float32)
    rhs = jnp.concatenate([v * beta[..., None], k_beta * jnp.exp(g)[..., None]], axis=-1)
    wu = lax.linalg.triangular_solve(eye + a_mat, rhs, left_side=True, lower=True,
                                     unit_diagonal=True)
    u, w = wu[..., :dv], wu[..., dv:]
    qk = jnp.where(causal, jnp.einsum("bhnck,bhndk->bhncd", q, k) * decay, 0.0)
    q_dec = q * jnp.exp(g)[..., None]
    g_last = g[..., -1]
    k_dec = k * jnp.exp(g_last[..., None] - g)[..., None]

    def step(s_state, xs):
        qk_i, q_dec_i, k_dec_i, u_i, w_i, gl_i = xs
        v_new = u_i - jnp.einsum("bhck,bhkv->bhcv", w_i, s_state)
        o = (jnp.einsum("bhck,bhkv->bhcv", q_dec_i, s_state)
             + jnp.einsum("bhcd,bhdv->bhcv", qk_i, v_new))
        s_state = (s_state * jnp.exp(gl_i)[..., None, None]
                   + jnp.einsum("bhck,bhcv->bhkv", k_dec_i, v_new))
        return s_state, o

    xs = tuple(jnp.moveaxis(a, 2, 0) for a in (qk, q_dec, k_dec, u, w, g_last))
    s0 = jnp.zeros((b, h, dk, dv), jnp.float32)
    _, o = lax.scan(step, s0, xs)
    return jnp.moveaxis(o, 0, 2).reshape(b, h, t, dv)

def hgrn2_recurrence(q, k, i_val, log_f):
    b, h, t, dk = q.shape
    dv = i_val.shape[-1]
    n = t // CHUNK
    rs = lambda a: a.reshape(b, h, n, CHUNK, a.shape[-1])
    q, k, i_val = rs(q), rs(k), rs(i_val)
    bcum = jnp.cumsum(rs(log_f), axis=-2)
    b_last = bcum[..., -1, :]
    q_dec = q * jnp.exp(bcum)
    k_dec = k * jnp.exp(b_last[..., None, :] - bcum)
    idx = jnp.arange(CHUNK)
    causal = (idx[:, None] >= idx[None, :])[:, :, None]

    def step(s_state, xs):
        q_i, k_i, v_i, b_i, q_dec_i, k_dec_i, bl_i = xs
        diff = b_i[:, :, :, None, :] - b_i[:, :, None, :, :]
        dec = jnp.exp(jnp.where(causal, diff, -jnp.inf))
        a_mat = jnp.einsum("bhtk,bhsk,bhtsk->bhts", q_i, k_i, dec)
        o = (jnp.einsum("bhtk,bhkv->bhtv", q_dec_i, s_state)
             + jnp.einsum("bhts,bhsv->bhtv", a_mat, v_i))
        s_state = (s_state * jnp.exp(bl_i)[..., None]
                   + jnp.einsum("bhsk,bhsv->bhkv", k_dec_i, v_i))
        return s_state, o

    xs = tuple(jnp.moveaxis(a, 2, 0) for a in (q, k, i_val, bcum, q_dec, k_dec, b_last))
    s0 = jnp.zeros((b, h, dk, dv), jnp.float32)
    _, o = lax.scan(step, s0, xs)
    return jnp.moveaxis(o, 0, 2).reshape(b, h, t, dv)

def fox_gdn_mixer(h, w_in, fox_q_norm, fox_k_norm, fox_f_bias, gdn_conv, gdn_A_log,
                  gdn_dt_bias, gdn_o_norm, w_out):
    b, t, _ = h.shape
    z = h @ w_in
    fq, fk, fv, ff, gq, gk, gv, gb, ga, gg = split_cols(z, EVEN_SPLIT)
    fq = rms_norm(fq.reshape(b, t, FOX_HEADS, FOX_HEAD_DIM), fox_q_norm)
    fk = rms_norm(fk.reshape(b, t, FOX_HEADS, FOX_HEAD_DIM), fox_k_norm)
    fv = fv.reshape(b, t, FOX_HEADS, FOX_HEAD_DIM)
    fox_o = forgetting_attention(fq, fk, fv, ff + fox_f_bias)
    fox_o = fox_o.reshape(b, t, FOX_W).astype(h.dtype)
    conv = jax.nn.silu(causal_depthwise_conv(jnp.concatenate([gq, gk, gv], axis=-1), gdn_conv))
    cq, ck, cv = split_cols(conv, (GDN_W, GDN_W, GDN_W))
    to_heads = lambda a: a.reshape(b, t, GDN_HEADS, GDN_HEAD_DIM).transpose(0, 2, 1, 3)
    q = to_heads(l2_normalize(cq.reshape(b, t, GDN_HEADS, GDN_HEAD_DIM)).reshape(b, t, GDN_W))
    k = to_heads(l2_normalize(ck.reshape(b, t, GDN_HEADS, GDN_HEAD_DIM)).reshape(b, t, GDN_W))
    v = to_heads(cv.astype(jnp.float32))
    beta = jax.nn.sigmoid(gb.astype(jnp.float32)).transpose(0, 2, 1)
    log_alpha = (-jnp.exp(gdn_A_log.astype(jnp.float32))
                 * jax.nn.softplus(ga.astype(jnp.float32) + gdn_dt_bias.astype(jnp.float32)))
    gdn_o = gated_delta_rule(q, k, v, log_alpha.transpose(0, 2, 1), beta)
    gdn_o = gdn_o.transpose(0, 2, 1, 3)
    gate = jax.nn.silu(gg.astype(jnp.float32)).reshape(b, t, GDN_HEADS, GDN_HEAD_DIM)
    gdn_o = (rms_norm(gdn_o, gdn_o_norm) * gate).reshape(b, t, GDN_W).astype(h.dtype)
    return jnp.concatenate([fox_o, gdn_o], axis=-1) @ w_out

def hgrn2_mixer(h, w_in, lower_bound, o_norm, w_out):
    b, t, _ = h.shape
    z = h @ w_in
    zq, zf, zi, zg = split_cols(z, (D_MODEL, D_MODEL, D_MODEL, D_MODEL))
    q = jax.nn.silu(zq.astype(jnp.float32))
    f = lower_bound + (1.0 - lower_bound) * jax.nn.sigmoid(zf.astype(jnp.float32))
    k = 1.0 - f
    log_f = jnp.log(f)
    to_heads = lambda a: a.reshape(b, t, HGRN_HEADS, HGRN_HEAD_DIM).transpose(0, 2, 1, 3)
    o = hgrn2_recurrence(to_heads(q), to_heads(k), to_heads(zi.astype(jnp.float32)),
                         to_heads(log_f))
    o = o.transpose(0, 2, 1, 3)
    gate = jax.nn.silu(zg.astype(jnp.float32)).reshape(b, t, HGRN_HEADS, HGRN_HEAD_DIM)
    o = (rms_norm(o, o_norm) * gate).reshape(b, t, D_MODEL).astype(h.dtype)
    return o @ w_out

def setup_inputs(seed: int = 0) -> dict:
    key = jax.random.key(seed)
    ks = jax.random.split(key, 24)
    f32 = jnp.float32

    def dense(k, fan_in, fan_out):
        return jax.random.normal(k, (fan_in, fan_out), f32) * fan_in ** -0.5

    def gain(k, n):
        return 1.0 + 0.1 * jax.random.normal(k, (n,), f32)

    dt = jnp.exp(jax.random.uniform(ks[8], (GDN_HEADS,), f32, math.log(1e-3), math.log(1e-1)))
    return {
        "x": jax.random.normal(ks[0], (BATCH, SEQ, D_MODEL), f32),
        "l0_mix_norm": gain(ks[1], D_MODEL),
        "l0_w_in": dense(ks[2], D_MODEL, EVEN_IN),
        "l0_fox_q_norm": gain(ks[3], FOX_HEAD_DIM),
        "l0_fox_k_norm": gain(ks[4], FOX_HEAD_DIM),
        "l0_fox_f_bias": FOX_F_BIAS_MEAN + 0.1 * jax.random.normal(ks[5], (FOX_HEADS,), f32),
        "l0_gdn_conv": jax.random.normal(ks[6], (GDN_CONV, 3 * GDN_W), f32) * GDN_CONV ** -0.5,
        "l0_gdn_A_log": jnp.log(jax.random.uniform(ks[7], (GDN_HEADS,), f32, 1.0, 16.0)),
        "l0_gdn_dt_bias": dt + jnp.log(-jnp.expm1(-dt)),
        "l0_gdn_o_norm": gain(ks[9], GDN_HEAD_DIM),
        "l0_w_out": dense(ks[10], FOX_W + GDN_W, D_MODEL),
        "l0_ffn_norm": gain(ks[11], D_MODEL),
        "l0_w_ff1": dense(ks[12], D_MODEL, D_FF),
        "l0_w_ff2": dense(ks[13], D_FF, D_MODEL),
        "l1_mix_norm": gain(ks[14], D_MODEL),
        "l1_w_in": dense(ks[15], D_MODEL, ODD_IN),
        "l1_hgrn_o_norm": gain(ks[16], HGRN_HEAD_DIM),
        "l1_w_out": dense(ks[17], D_MODEL, D_MODEL),
        "l1_ffn_norm": gain(ks[18], D_MODEL),
        "l1_w_ff1": dense(ks[19], D_MODEL, D_FF),
        "l1_w_ff2": dense(ks[20], D_FF, D_MODEL),
        "hgrn_lb_logits": 0.5 * jax.random.normal(ks[21], (DEPTH, D_MODEL), f32),
    }

def reference(x, l0_mix_norm, l0_w_in, l0_fox_q_norm, l0_fox_k_norm, l0_fox_f_bias,
              l0_gdn_conv, l0_gdn_A_log, l0_gdn_dt_bias, l0_gdn_o_norm, l0_w_out,
              l0_ffn_norm, l0_w_ff1, l0_w_ff2, l1_mix_norm, l1_w_in, l1_hgrn_o_norm,
              l1_w_out, l1_ffn_norm, l1_w_ff1, l1_w_ff2, hgrn_lb_logits):
    lb_soft = jax.nn.softmax(hgrn_lb_logits.astype(jnp.float32), axis=0)
    lower_bounds = jnp.cumsum(lb_soft, axis=0) - lb_soft[0]
    layers = (
        dict(mix_norm=l0_mix_norm, ffn_norm=l0_ffn_norm, w_ff1=l0_w_ff1, w_ff2=l0_w_ff2),
        dict(mix_norm=l1_mix_norm, ffn_norm=l1_ffn_norm, w_ff1=l1_w_ff1, w_ff2=l1_w_ff2),
    )
    for l in range(DEPTH):
        p = layers[l]
        h = rms_norm(x, p["mix_norm"])
        if l % 2 == 0:
            mix = fox_gdn_mixer(h, l0_w_in, l0_fox_q_norm, l0_fox_k_norm, l0_fox_f_bias,
                                l0_gdn_conv, l0_gdn_A_log, l0_gdn_dt_bias, l0_gdn_o_norm,
                                l0_w_out)
        else:
            mix = hgrn2_mixer(h, l1_w_in, lower_bounds[l], l1_hgrn_o_norm, l1_w_out)
        x = x + mix.astype(x.dtype)
        x = x + squared_relu_mlp(rms_norm(x, p["ffn_norm"]), p["w_ff1"], p["w_ff2"]).astype(x.dtype)
    return x


_drawn_inputs = setup_inputs


def setup_inputs(seed=0):
    import zlib

    import numpy as np

    out = dict(_drawn_inputs(seed))
    spreads = {}
    factors = {'l0_fox_f_bias': 28.88,
     'hgrn_lb_logits': 2.89,
     'l0_fox_q_norm': 4.559,
     'l0_fox_k_norm': 5.426}
    for name, (base, spread) in spreads.items():
        noise = np.random.default_rng([zlib.crc32(name.encode()), seed]).standard_normal(out[name].shape)
        drawn = base * np.exp(spread * noise) if base else spread * noise
        out[name] = jnp.asarray(drawn.astype(out[name].dtype))
    for name, factor in factors.items():
        out[name] = (out[name] * factor).astype(out[name].dtype)
    return out
```

```python
import concourse.bass as bass
import numpy as np
from concourse import mybir

F32 = mybir.dt.float32
F32R = mybir.dt.float32r
BF16 = mybir.dt.bfloat16
U32 = mybir.dt.uint32
ALU = mybir.AluOpType
ACT = mybir.ActivationFunctionType
AX = mybir.AxisListType

P = 128
T = 512
D = 1024
KB = D // P
TT = T // P
CHUNK = 64
NCH = T // CHUNK
FF = 4 * D
QUARTERS = FF // D
FOX_HEADS, FOX_DH = 8, 64
GDN_HEADS, DH = 4, 128
FOX_W, GDN_W = FOX_HEADS * FOX_DH, GDN_HEADS * DH
HG_HEADS = 8
EPS = 1e-6
NEG = -1.0e30

O_FQ, O_FK, O_FV, O_FF = 0, FOX_W, 2 * FOX_W, 3 * FOX_W
O_GQ = O_FF + FOX_HEADS
O_GK, O_GV = O_GQ + GDN_W, O_GQ + 2 * GDN_W
O_GB = O_GQ + 3 * GDN_W
O_GA = O_GB + GDN_HEADS
O_GG = O_GA + GDN_HEADS
R_F, R_B, R_A, ROWS = 0, 32, 64, 96

LEVELS = 6

_c = {}


def _cols(names):
    at = 0
    for name, width in names:
        _c[name] = (at, width)
        at += width
    return at


CONST_W = _cols([("ident", P), ("causal_neg", P), ("strict", P), ("fox_neg", P), ("ones", P), ("pair_ones", P)]
                + [(f"low{b}", P) for b in range(LEVELS)] + [(f"up{b}", P) for b in range(LEVELS)]
                + [("chunk_reset", T)])
_c["row_reset"] = (CONST_W, T)
_p = {}
_at = 0
for _n, _w in [("g0", KB), ("g1", KB), ("g2", KB), ("g3", KB), ("fqn", 1), ("fkn", 1), ("gdn_o", 1), ("hg_o", 1),
               ("conv", 4 * 3 * GDN_HEADS), ("lb0", HG_HEADS), ("lb1", HG_HEADS), ("row_bias", 1), ("row_a", 1),
               ("row_sign", 1), ("eps", 1)]:
    _p[_n] = (_at, _w)
    _at += _w
PARAM_W = _at


def constants():
    r, c = np.arange(P)[:, None], np.arange(P)[None, :]
    same = r // CHUNK == c // CHUNK
    out = np.zeros((P, CONST_W + T), np.float32)

    def put(name, a):
        at, w = _c[name]
        out[:, at:at + w] = a

    put("ident", r == c)
    put("causal_neg", np.where(same & (c >= r), 0.0, NEG))
    put("strict", same & (c > r))
    put("fox_neg", np.where(c > r, NEG, 0.0))
    put("ones", 1.0)
    put("pair_ones", r // FOX_DH == c // FOX_DH)
    for b in range(LEVELS):
        h = 1 << b
        block = r // (2 * h) == c // (2 * h)
        low = block & (r % (2 * h) >= h) & (c % (2 * h) < h)
        put(f"low{b}", low)
        put(f"up{b}", low.T)
    t = np.arange(T)[None, :]
    put("chunk_reset", (t % CHUNK != 0))
    put("row_reset", np.where(np.arange(P)[:, None] < R_A, 1.0, (t % CHUNK != 0)))
    return out


class Signal:

    def __init__(self, sem, per, first=0):
        self.sem, self.per, self.first = sem, per, first

    def __call__(self, i, k=None):
        return self.sem, i * self.per + (self.first + (self.per if k is None else k))


EXP_LN = "natural_log_exp_and_others"
LEAD = 3
RAW, SPLIT = 8, 4


class Phase:

    def __init__(self, passes, tiles, raw_slots, before):
        self.passes, self.tiles, self.raw_slots = passes, tiles, raw_slots
        self.base = before.base + before.passes * before.tiles if before else 0
        self.uses = list(before.uses_after()) if before else [0] * RAW
        self.before = before

    def uses_after(self):
        return [u + self.passes * sum(1 for j in range(self.tiles) if j % self.raw_slots == s)
                for s, u in enumerate(self.uses)]

    def n(self, p, j):
        return p * self.tiles + (self.base + j)

    def raw(self, j):
        return j % self.tiles % self.raw_slots

    def split(self, j):
        return j % self.tiles % SPLIT

    def arrivals(self, p, j):
        extra, j = divmod(j, self.tiles)
        s = j % self.raw_slots
        per = sum(1 for x in range(self.tiles) if x % self.raw_slots == s)
        return (p + extra) * per + (self.uses[s] + j // self.raw_slots + 1)

    def split_back(self, j):
        j = j % self.tiles
        pat = [self.split(x) for x in range(self.tiles)] * 3
        at = j + 2 * self.tiles
        return next(d for d in range(1, 2 * self.tiles + 1) if pat[at - d] == pat[at])


PH_L0 = Phase(GDN_HEADS, 7, 7, None)
PH_OUT0 = Phase(1, 8, 8, PH_L0)
PH_MLP0 = Phase(QUARTERS, 16, 8, PH_OUT0)
PH_L1 = Phase(HG_HEADS, 4, 4, PH_MLP0)
PH_OUT1 = Phase(1, 8, 8, PH_L1)
PH_MLP1 = Phase(QUARTERS, 16, 8, PH_OUT1)
TILES = PH_MLP1.base + PH_MLP1.passes * PH_MLP1.tiles



def schedule(slots, *chains):
    at = [[] for _ in range(slots)]
    for chain in chains:
        for step, slot in chain:
            at[min(slot, slots - 1)].append(step)
    return at


L0_SLICES = 7 * KB
_gdn = [(("conv",), 0), (("gdn_norm",), 11), (("gdn_gate",), 13), (("gdn_gram",), 15), (("inv0",), 18)]
_slot = 20.0
for _l in range(1, LEVELS):
    _gdn += [(("inv_a", _l), int(_slot)), (("inv_b", _l), int(_slot + 1.5))]
    _slot += 3
_gdn += [(("uw",), int(_slot))]
_slot += 2
for _n in range(NCH):
    if _n:
        _gdn += [(("scan_v", _n), int(_slot))]
        _slot += 1.15
    _gdn += [(("scan_s", _n), int(_slot))]
    _slot += 1.15
_gdn += [(("gdn_out",), 55)]
_fox = [(("fox_norm",), 2)]
for _u in range(8):
    _s = 8 + 5 * _u
    _fox += [(("fox_s", _u), _s)]
    if _u:
        _fox += [(("fox_t", _u - 1), _s + 1), (("fox_o", _u - 1), _s + 3)]
_fox += [(("fox_t", 7), 48), (("fox_o", 7), 50), (("fox_out",), 52)]
MIX0 = schedule(L0_SLICES, _gdn, _fox)

L1_SLICES = 4 * KB
_hg = [(("hg_gates",), 0), (("hg_diag",), 6)]
for _l in range(LEVELS):
    _hg += [(("hg_level", _l), 8 + 2 * _l)]
_hg += [(("hg_kv",), 20), (("hg_o",), 24), (("hg_norm",), 28)]
MIX1 = schedule(L1_SLICES, _hg)


def build(nc, x, w_in0, w_out0, w_ff1_0, w_ff2_0, w_in1, w_out1, w_ff1_1, w_ff2_1, params, consts, out):
    spill = nc.dram_tensor("residual_spill", (P, KB * T), F32).ap()
    rows_dram = nc.dram_tensor("gate_rows", (ROWS, T), F32).ap()

    at = [(nc.sbuf_base + 31) // 32 * 32]

    def place(name, shape, dtype, here=None):
        size = (4 if dtype != BF16 else 2) * int(np.prod(shape[1:]))
        size = (size + 31) // 32 * 32
        spot = at if here is None else here
        t = nc.alloc_sbuf_tensor_at(name, list(shape), dtype, offset=spot[0])
        spot[0] += size
        return t

    h_hi = place("h_hi", [P, KB, T], F32R)
    h_lo = place("h_lo", [P, KB, T], F32R)
    a_hi = place("a_hi", [P, KB, T], F32R)
    a_lo = place("a_lo", [P, KB, T], F32R)
    raw = place("w_raw", [P, RAW, KB, P], F32)
    w_hi = place("w_hi", [P, SPLIT, KB, P], F32R)
    w_lo = place("w_lo", [P, SPLIT, KB, P], F32R)
    cst = place("consts", [P, CONST_W], F32)
    par = place("params", [P, PARAM_W], F32)
    rstd = place("rstd", [P, T], F32)
    neg_b = place("fox_neg_b", [P, P], BF16)
    ident_b = place("ident_b", [P, P], BF16)
    nat = place("rows_nat", [P, TT, ROWS], F32)
    kb_scale = place("kb_scale", [P, TT, GDN_HEADS], F32)
    kd_scale = place("kd_scale", [P, TT, GDN_HEADS], F32)
    small = place("small", [P, 16], F32)
    lbs = place("lower_bound", [P, 4, HG_HEADS], F32)

    xt_at = at[0]
    xT = place("xT", [P, KB, T], F32)
    mix_at = at[0]

    def cc(name):
        a, w = _c[name]
        return cst[:, a:a + w]

    def pp(name, k=0, n=1):
        a, _ = _p[name]
        return par[:, a + k:a + k + n]

    m = [mix_at]
    xn = place("x_nat", [P, TT, D], F32, m)
    wsm = place("w_small", [P, KB, ROWS], F32, m)
    wsm_hi = place("w_small_hi", [P, KB, ROWS], F32R, m)
    wsm_lo = place("w_small_lo", [P, KB, ROWS], F32R, m)
    row = [place(f"row{i}", [ROWS, T], F32, m) for i in range(4)]
    row_reset = place("row_reset", [P, T], F32, m)
    assert m[0] <= mix_at + 38 * 1024
    m = [mix_at + 38 * 1024]
    sq = [place(f"sq{i}", [P, T], F32, m) for i in range(2)]
    ssq = place("ssq", [P, T], F32, m)
    m = [mix_at]
    relu = [place(f"relu{i}", [P, T], F32, m) for i in range(2)]
    act2 = [place(f"act2_{i}", [P, T], F32, m) for i in range(2)]
    yn = place("y_nat", [P, 2, TT, P], F32, m)
    m = [xt_at]
    cqkv = [place(f"conv_{s}", [P, T], F32, m) for s in "qkv"]
    g_bc = place("g_bc", [P, T], F32, m)
    b_bc = place("beta_bc", [P, T], F32, m)
    c_bc = [place(f"c_bc{i}", [P, T], F32, m) for i in range(2)]
    qd = place("q_dec", [P, T], F32, m)
    assert m[0] <= mix_at
    m[0] = mix_at
    z0 = [place(f"z_{s}", [P, 3 + T] if s[0] == "g" and s != "gg" else [P, T], F32, m)
          for s in ("gq", "gk", "gv", "fq", "fk", "fv", "gg")]
    assert m[0] <= mix_at + TT * D * 4
    kbeta = place("k_beta", [P, T], F32, m)
    dmat = place("decay", [P, TT, P], F32, m)
    vb = place("v_beta", [P, TT, P], F32, m)
    kbg = place("kb_g", [P, TT, P], F32, m)
    kdec = place("k_dec", [P, TT, P], F32, m)
    nmat = place("n_mat", [P, TT, P], F32, m)
    qkT = place("qkT", [P, TT, P], F32, m)
    gate = place("gate", [P, T], F32, m)
    fqn = place("fqn", [P, T], F32, m)
    fkn = place("fkn", [P, T], F32, m)
    fvn = place("fv_nat", [P, TT, P], F32, m)
    prob = [place(f"prob{i}", [P, T], F32, m) for i in range(2)]
    probT = place("probT", [P, TT, P], F32, m)
    state = place("state", [P, P], F32, m)
    xm = kbeta
    ym = place("inv_t", [P, TT, P], F32, m)
    pm = place("inv_p", [P, TT, P], F32, m)
    dstr = pm
    xmv = xm[:, :].rearrange("p (t c) -> p t c", c=P)
    print("SBUF end of layer 0 mixers:", m[0])
    m = [mix_at]
    z1 = [place(f"z1_{s}", [P, T], F32, m) for s in "qfig"]
    hq = place("h_q", [P, T], F32, m)
    hk = place("h_k", [P, T], F32, m)
    hf = place("h_f", [P, T], F32, m)
    hb = place("h_b", [P, T], F32, m)
    hdec = place("h_dec", [P, T], F32, m)
    hqd = place("h_qd", [P, T], F32, m)
    hkd = place("h_kd", [P, T], F32, m)
    hv = place("h_v", [P, TT, P], F32, m)
    hkn = place("h_kn", [P, TT, P], F32, m)
    he = [place(f"h_e{i}", [P, T], F32, m) for i in range(2)]
    hx = [place(f"h_x{i}", [P, T], F32, m) for i in range(2)]
    hA = place("h_A", [P, TT, P], F32, m)
    hS = place("h_S", [P, NCH, P], F32, m)
    hg = place("h_gate", [P, T], F32, m)
    print("SBUF end of layer 1 mixers:", m[0], "limit", nc.sbuf_usable_end)
    ho = he[0]
    ht = hx[0]

    def bank(name):
        return nc.alloc_psum_tensor(name, [P, T], F32)

    dense = [bank("dense0"), bank("dense1")]
    mb = [bank(f"mix{i}") for i in range(6)]
    g0, g1, g2, f0, f1, f2 = mb

    sems = {}

    def sig(name, per=1, first=0):
        if name not in sems:
            sems[name] = nc.alloc_semaphore(name)
        return Signal(sems[name], per, first)

    def t4(a):
        return a[:, :].rearrange("p (t c) -> p t c", c=P)

    raw_in = [sig(f"raw_in{s}") for s in range(RAW)]
    hi_done = sig("w_hi_done")
    lo_done = sig("w_lo_done")
    gemm_done = sig("gemm_done")
    evac_done = sig("evac_done")
    const_in = sig("const_in")
    x_in = sig("x_in")
    par_in = sig("params_in")
    wsm_z = sig("w_small_zeroed")
    wsm_in = sig("w_small_in")
    xtr = sig("x_transposed", KB)
    x_ev = sig("x_evacuated", KB)
    b_const = sig("bf16_consts", 2)
    h_hi_s = sig("h_hi_ready", KB)
    h_sq = sig("h_squares", KB)
    h_lo_s = sig("h_lo_ready", KB)
    ssq_s = sig("squares_summed", KB)
    stat_mm = sig("stat_mm")
    stat_ln = sig("stat_ln")
    rstd_s = sig("rstd_ready")
    wsm_hi_s, wsm_lo_s = sig("w_small_hi_s"), sig("w_small_lo_s")
    row_mm = sig("row_mm")
    row_v = sig("row_vector", 9)
    row_a = sig("row_scalar", 8)
    row_tr = sig("row_transposed", 2)
    row_out = sig("rows_written")
    spilled = sig("x_spilled")
    reloaded = sig("x_reloaded")
    pads = sig("conv_pads", 3)
    z0_s = [sig(f"projected{i}") for i in range(7)]
    g_in, b_in, c_in = sig("g_bc_in"), sig("beta_bc_in"), [sig("c0_in"), sig("c1_in")]
    conv_s = sig("conv", 12)
    silu_s = sig("silu", 4)
    gsq = sig("gdn_squares", 2)
    fsq = sig("fox_squares", 2)
    gn_mm, gn_ln, gn_r, gn = sig("gdn_norm_mm", 2), sig("gdn_norm_ln", 2), sig("gdn_norm_r", 2), sig("gdn_normed", 2)
    fn_mm, fn_ln, fn_r, fn = sig("fox_norm_mm", 2), sig("fox_norm_ln", 2), sig("fox_norm_r", 2), sig("fox_normed", 2)
    kbeta_s, darg_s, dexp_s, eg_s, qd_s, dstr_s = (sig("k_beta_s"), sig("decay_arg", TT), sig("decay_exp"),
                                                  sig("exp_g"), sig("q_dec_s"), sig("decay_strict_s"))
    k_tr, v_tr, fv_tr, fv_ev = sig("k_tr"), sig("v_tr"), sig("fv_tr"), sig("fv_nat_s")
    k_nat, vb_s = sig("k_nat", 2), sig("vb_s")
    gram, n_s, qkT_s = sig("gram", 2), sig("n_mat_s"), sig("qkT_s")
    inv_a, inv_p, inv_x, inv_y = sig("inv_a", LEVELS), sig("inv_p_s", 5), sig("inv_x", 4), sig("inv_y", 5)
    x_0, y_0, x_up, y_up = sig("x_0", 2), sig("y_0", 2), sig("x_up", 4), sig("y_up", 5)
    u_mm, w_mm, u_ev, w_ev = sig("u_mm"), sig("w_mm"), sig("u_ev"), sig("w_ev")
    sv_mm, vnew, ss_mm, so_mm, s_up = (sig("scan_v_mm", NCH - 1), sig("v_new", NCH), sig("scan_s_mm", NCH - 1),
                                       sig("scan_o_mm", NCH), sig("state_up", NCH - 1))
    go_sq, go_mm, go_ln, go_r, go_n, go_g, go_hi, go_lo = [sig(f"mix_out_{s}") for s in
                                                         ("sq", "mm", "ln", "r", "n", "g", "hi", "lo")]
    fs_mm, fs_s, fs_m, fs_nm, fs_e, fs_r, fs_p = [sig(f"fox_{s}", 8) for s in
                                                  ("s_mm", "s", "max", "negmax", "exp", "recip", "prob")]
    ft_mm, ft_c, fo_mm = sig("fox_t_mm", 8), sig("fox_t_c", 8), sig("fox_o_mm", 8)
    fo_hi, fo_lo = sig("fox_out_hi"), sig("fox_out_lo")
    pe_mix0, act_mix0, dve_mix0, pool_mix0 = [sig(f"{e}_mix_done") for e in ("pe", "act", "dve", "pool")]
    relu_s, sq_s, ahi_s, alo_s = [[sig(n, KB, l * KB * QUARTERS) for l in range(2)]
                                    for n in ("relu", "relu2", "a_hi", "a_lo")]
    resid = [sig("residual", KB, l * KB * QUARTERS) for l in range(2)]
    x_out = [sig("x_after_mix", KB, l * KB) for l in range(2)]
    z1_s = [sig(f"projected{i}", 1, GDN_HEADS) for i in range(4)]
    lb_a, lb_v = sig("lb_scalar", 2), sig("lb_vector", 8)
    hq_s, hg_s, hexp_s, hd_s, hr_s, hf_s, hk_s, hln_s, hb_s = [sig(f"hg_{s}") for s in
        ("q", "gate", "exp", "den", "rec", "f", "k", "ln", "b")]
    heb_s, hqd_s, hka_s, hke_s, hkd_s = [sig(f"hg_{s}") for s in ("eb", "qd", "karg", "kexp", "kd")]
    hv_tr, hv_s, hkn_tr, hkn_s, hdg_mm, hdg_s = [sig(f"hg_{s}") for s in ("v_tr", "v", "kn_tr", "kn", "diag_mm", "diag")]
    hl_d, hl_e, hl_x, hl_mm, hl_c = (sig("hgl_arg", 12), sig("hgl_exp", 6), sig("hgl_x", 12), sig("hgl_mm", 6),
                                     sig("hgl_copy", 6))
    hkv_mm, hS_s, ho_mm = sig("hg_kv_mm", 2), sig("hg_S", NCH - 1), sig("hg_o_mm")
    ho_sq, hn_mm, hn_ln, hn_r, hn_t, hn_g, hn_hi, hn_lo = [sig(f"mix_out_{s}", 1, GDN_HEADS) for s in
                                                           ("sq", "mm", "ln", "r", "n", "g", "hi", "lo")]
    pe_mix1, act_mix1, dve_mix1, pool_mix1 = [sig(f"{e}_mix_done", 1, GDN_HEADS) for e in ("pe", "act", "dve", "pool")]
    y_tr, y_ev = sig("y_transposed", KB), sig("y_evacuated", KB)
    stored = [sig("stored0"), sig("stored1")]
    print("semaphores:", len(sems))

    def gain(use):
        return f"g{use}"

    def load(sp, ph, p, j, src, back):
        if back is not None:
            sp.wait_ge(lo_done.sem, ph.n(p, j) - (back - 1))
        sp.dma_start(raw[:, ph.raw(j)], src).then_inc(raw_in[ph.raw(j)].sem, 16)

    def split_hi(act, ph, p, j):
        act.wait_ge(raw_in[ph.raw(j)].sem, 16 * ph.arrivals(p, j))
        first = isinstance(p, int) and ph.n(p, j) < SPLIT
        if not first:
            act.wait_ge(gemm_done.sem, ph.n(p, j) - (back_of(ph, j) - 1))
        act.activation(w_hi[:, ph.split(j)], raw[:, ph.raw(j)], ACT.Copy).then_inc(hi_done.sem, 1)

    def back_of(ph, j):
        if ph is PH_OUT0 and j < SPLIT:
            return [3, 3, 3, 7][j]
        return ph.split_back(j)

    def split_lo(dve, ph, p, j):
        dve.wait_ge(hi_done.sem, ph.n(p, j) + 1)
        dve.tensor_tensor(w_lo[:, ph.split(j)], raw[:, ph.raw(j)], w_hi[:, ph.split(j)].bitcast(F32),
                          ALU.subtract).then_inc(lo_done.sem, 1)

    def products(pe, ph, p, j, k, xhi, xlo, ready):
        n, s = ph.n(p, j), ph.split(j)
        if k == 0:
            pe.wait_ge(lo_done.sem, n + 1)
            if not (isinstance(n, int) and n < 2):
                prev = 0 if (ph is PH_L0 and j == 0) else 1
                pe.wait_ge(evac_done.sem, n - prev)
        if ready is not None:
            pe.wait_ge(*ready(k))
        b = dense[j % 2]
        pe.matmul(b[:, :], w_hi[:, s, k], xhi[:, k], start=(k == 0), stop=False)
        pe.matmul(b[:, :], w_lo[:, s, k], xhi[:, k], start=False, stop=False)
        last = pe.matmul(b[:, :], w_hi[:, s, k], xlo[:, k], start=False, stop=(k == KB - 1))
        if k == KB - 1:
            last.then_inc(gemm_done.sem, 1)

    block = nc.Block()
    with block:

        @block.sync
        def _(sp):
            sp.dma_start(xn[:, :, :], x.rearrange("o (t p) d -> p (o t) d", p=P)).then_inc(x_in.sem, 16)
            sp.dma_start(cst[:, :], consts[:, 0:CONST_W]).then_inc(const_in.sem, 16)
            sp.dma_start(par[:, :], params).then_inc(par_in.sem, 16)
            sp.dma_start(row_reset[:, :], consts[:, CONST_W:CONST_W + T]).then_inc(par_in.sem, 16)
            sp.wait_ge(*wsm_z(0))
            for r, o, w in ((R_F, O_FF, FOX_HEADS), (R_B, O_GB, GDN_HEADS), (R_A, O_GA, GDN_HEADS)):
                sp.dma_start(wsm[:, :, r:r + w], w_in0[:, o:o + w].rearrange("(k p) c -> p k c", p=P))\
                    .then_inc(wsm_in.sem, 16)
            tile_of = lambda w, r0, c0: w[bass.ds(r0, D), bass.ds(c0, P)].rearrange("(k p) c -> p k c", p=P)
            starts = (O_GQ, O_GK, O_GV, O_FQ, O_FK, O_FV, O_GG)
            for j, o in enumerate(starts):
                load(sp, PH_L0, 0, j, tile_of(w_in0, 0, o), None)
            sp.wait_ge(*h_sq(0))
            sp.wait_ge(*h_lo_s(0))
            sp.dma_start(spill, xT[:, :, :].rearrange("p k t -> p (k t)")).then_inc(spilled.sem, 16)
            sp.wait_ge(*row_v(0, 7))
            sp.wait_ge(*row_a(0, 5))
            sp.dma_start(rows_dram, row[0][:, :]).then_inc(row_out.sem, 16)
            with sp.Fori(1, GDN_HEADS) as p:
                for j in (0, 1, 2, 4, 3, 5, 6):
                    load(sp, PH_L0, p, j, tile_of(w_in0, 0, p * P + starts[j]), 7 if j != 3 else None)
            for layer, (ph_o, ph_m, w_out, w1, w2) in enumerate(((PH_OUT0, PH_MLP0, w_out0, w_ff1_0, w_ff2_0),
                                                                 (PH_OUT1, PH_MLP1, w_out1, w_ff1_1, w_ff2_1))):
                if layer:
                    col = lambda g, h: tile_of(w_in1, 0, h * P + g * D)
                    with sp.Fori(0, HG_HEADS) as p:
                        for j, g in enumerate((0, 1, 2, 3)):
                            load(sp, PH_L1, p, j, col(g, p), 4)
                for j in range(KB):
                    back = (7 if j < 7 else None) if layer == 0 else (4 if j < 4 else 36)
                    load(sp, ph_o, 0, j, tile_of(w_out, 0, j * P), back)
                if layer == 0:
                    for s in (pe_mix0, act_mix0, dve_mix0, pool_mix0):
                        sp.wait_ge(*s(GDN_HEADS, 1))
                    sp.dma_start(xT[:, :, :].rearrange("p k t -> p (k t)"), spill).then_inc(reloaded.sem, 16)
                with sp.Fori(0, QUARTERS) as q:
                    for j in range(KB):
                        load(sp, ph_m, q, j, tile_of(w1, 0, q * D + j * P), 8)
                    for j in range(KB):
                        load(sp, ph_m, q, KB + j, tile_of(w2, q * D, j * P), 8)
            for d in range(KB):
                sp.wait_ge(*y_ev(0, d + 1))
                sp.dma_start(out[0].rearrange("(t p) d -> p t d", p=P)[:, :, d * P:(d + 1) * P],
                             yn[:, d % 2]).then_inc(stored[d % 2].sem, 16)
            for s in stored:
                sp.wait_ge(s.sem, 16 * KB // 2)
            sp.wait_ge(spilled.sem, 16)
            sp.wait_ge(row_out.sem, 16)

        @block.tensor
        def _(pe):
            ident = cc("ident")
            pe.wait_ge(const_in.sem, 16)
            pe.wait_ge(x_in.sem, 16)
            pe.wait_ge(*b_const(0))
            for k in range(KB):
                if k >= 2:
                    pe.wait_ge(*x_ev(0, k - 1))
                for t in range(TT):
                    last = pe.transpose(mb[k % 2][:, t * P:(t + 1) * P], xn[:, t, k * P:(k + 1) * P], ident)
                last.then_inc(xtr.sem, 1)

            def stat(use):
                pe.wait_ge(*ssq_s(use))
                if use == 0:
                    pe.wait_ge(*x_ev(0))
                pe.matmul(g0[:, :], cc("ones"), ssq[:, :], start=True, stop=True).then_inc(stat_mm.sem, 1)

            stat(0)
            pe.wait_ge(*h_lo_s(0))
            pe.wait_ge(*wsm_lo_s(0))
            for k in range(KB):
                pe.matmul(g1[0:ROWS, :], wsm_hi[:, k], h_hi[:, k], start=(k == 0), stop=False)
                pe.matmul(g1[0:ROWS, :], wsm_lo[:, k], h_hi[:, k], start=False, stop=False)
                last = pe.matmul(g1[0:ROWS, :], wsm_hi[:, k], h_lo[:, k], start=False, stop=(k == KB - 1))
            last.then_inc(row_mm.sem, 1)

            def project0(p, mix=None):
                for s in range(L0_SLICES):
                    products(pe, PH_L0, p, s // KB, s % KB, h_hi, h_lo, None)
                    if mix is not None:
                        for step, *arg in MIX0[s]:
                            if step in pe0:
                                pe0[step](mix, *arg)

            def gdn_norm(i):
                for n, b in ((0, g0), (1, g1)):
                    pe.wait_ge(*gsq(i, n + 1))
                    if n == 0:
                        pe.wait_ge(*dve_mix0(i, 1))
                        pe.wait_ge(*act_mix0(i, 1))
                    pe.matmul(b[:, :], cc("ones"), (xm, ym)[n][:, :] if n == 0 else ym[:, :, :], start=True, stop=True)\
                        .then_inc(gn_mm.sem, 1)

            def fox_norm(i):
                pe.wait_ge(*dve_mix0(i, 1))
                pe.wait_ge(*act_mix0(i, 1))
                for n, b in ((0, f0), (1, f1)):
                    pe.wait_ge(*fsq(i, n + 1))
                    pe.matmul(b[:, :], cc("pair_ones"), prob[n][:, :], start=True, stop=True).then_inc(fn_mm.sem, 1)
                pe.wait_ge(*z0_s[5](i))
                for t in range(TT):
                    last = pe.transpose(f2[:, t * P:(t + 1) * P], z0[5][:, t * P:(t + 1) * P], ident)
                last.then_inc(fv_tr.sem, 1)

            def gdn_gram(i):
                pe.wait_ge(*gn_r(i))
                pe.wait_ge(*gn(i))
                for t in range(TT):
                    last = pe.transpose(g2[:, t * P:(t + 1) * P], cqkv[1][:, t * P:(t + 1) * P], ident)
                last.then_inc(k_tr.sem, 1)
                pe.wait_ge(*silu_s(i, 4))
                for t in range(TT):
                    last = pe.transpose(g0[:, t * P:(t + 1) * P], cqkv[2][:, t * P:(t + 1) * P], ident)
                last.then_inc(v_tr.sem, 1)
                pe.wait_ge(*kbeta_s(i))
                for t in range(TT):
                    c = slice(t * P, (t + 1) * P)
                    last = pe.matmul(g1[:, c], cqkv[1][:, c], kbeta[:, c], start=True, stop=True)
                last.then_inc(gram.sem, 1)
                pe.wait_ge(*k_nat(i))
                for t in range(TT):
                    c = slice(t * P, (t + 1) * P)
                    last = pe.matmul(g2[:, c], cqkv[1][:, c], cqkv[0][:, c], start=True, stop=True)
                last.then_inc(gram.sem, 1)

            def inv0(i):
                pe.wait_ge(*n_s(i))
                pe.wait_ge(*vb_s(i))
                for t in range(TT):
                    last = pe.matmul(g0[:, t * P:(t + 1) * P], nmat[:, t], ident, start=True, stop=True)
                last.then_inc(inv_a.sem, 1)

            def inv_pa(i, l):
                if l == 1:
                    pe.wait_ge(*x_0(i))
                else:
                    pe.wait_ge(*x_up(i, l - 1))
                for t in range(TT):
                    last = pe.matmul(g0[:, t * P:(t + 1) * P], nmat[:, t], xmv[:, t], start=True, stop=True)
                last.then_inc(inv_a.sem, 1)

            def inv_pb(i, l):
                pe.wait_ge(*inv_p(i, l))
                if l == 1:
                    pe.wait_ge(*y_0(i))
                    pe.wait_ge(*qkT_s(i))
                else:
                    pe.wait_ge(*y_up(i, l - 1))
                if l < LEVELS - 1:
                    for t in range(TT):
                        last = pe.matmul(g1[:, t * P:(t + 1) * P], ym[:, t], pm[:, t], start=True, stop=True)
                    last.then_inc(inv_x.sem, 1)
                for t in range(TT):
                    last = pe.matmul(g2[:, t * P:(t + 1) * P], pm[:, t], ym[:, t], start=True, stop=True)
                last.then_inc(inv_y.sem, 1)

            def uw(i):
                pe.wait_ge(*y_up(i))
                for t in range(TT):
                    last = pe.matmul(g0[:, t * P:(t + 1) * P], ym[:, t], vb[:, t], start=True, stop=True)
                last.then_inc(u_mm.sem, 1)
                for t in range(TT):
                    last = pe.matmul(g1[:, t * P:(t + 1) * P], kbg[:, t], ym[:, t], start=True, stop=True)
                last.then_inc(w_mm.sem, 1)

            def scan_v(i, n):
                r = n % 2 * CHUNK
                pe.wait_ge(*s_up(i, n))
                if n == 1:
                    pe.wait_ge(*u_ev(i))
                pe.matmul(g0[r:r + CHUNK, 0:P], pm[:, n // 2, r:r + CHUNK], state[:, :], start=True, stop=True)\
                    .then_inc(sv_mm.sem, 1)

            def scan_s(i, n):
                r, t = n % 2 * CHUNK, n // 2
                c = slice(n * CHUNK, (n + 1) * CHUNK)
                if n:
                    pe.matmul(g2[:, c], state[:, :], qd[:, c], start=True, stop=False)
                pe.wait_ge(*vnew(i, n + 1))
                pe.matmul(g2[:, c], vnv[r:r + CHUNK, t], qkT[r:r + CHUNK, t, r:r + CHUNK], start=(n == 0), stop=True)\
                    .then_inc(so_mm.sem, 1)
                if n < NCH - 1:
                    if n == 0:
                        pe.wait_ge(*w_ev(i))
                    pe.matmul(g1[:, 0:P], kdec[r:r + CHUNK, t], vnv[r:r + CHUNK, t], start=True, stop=True)\
                        .then_inc(ss_mm.sem, 1)

            vnv = t4(cqkv[2])

            def gdn_out(i):
                pe.wait_ge(*go_sq(i))
                pe.matmul(g0[:, :], cc("ones"), xm[:, :], start=True, stop=True).then_inc(go_mm.sem, 1)

            def fox_s(i, u):
                hh, j = u // TT, u % TT
                h = slice(hh * FOX_DH, (hh + 1) * FOX_DH)
                if u == 0:
                    pe.wait_ge(*fn(i))
                else:
                    pe.wait_ge(*fs_s(i, u))
                n = (j + 1) * P
                pe.matmul(f0[:, 0:n], fqn[h, j * P:n], fkn[h, 0:n], start=True, stop=False)
                pe.matmul(f0[:, j * P:n], ident_b[:, :], neg_b[:, :], start=False, stop=True).then_inc(fs_mm.sem, 1)

            def fox_t(i, u):
                j = u % TT
                pe.wait_ge(*fs_p(i, u + 1))
                if u:
                    pe.wait_ge(*ft_c(i, u))
                for t in range(j + 1):
                    c = slice(t * P, (t + 1) * P)
                    last = pe.transpose(f1[:, c], prob[u % 2][:, c], ident)
                last.then_inc(ft_mm.sem, 1)

            def fox_o(i, u):
                hh, j = u // TT, u % TT
                h = slice(hh * FOX_DH, (hh + 1) * FOX_DH)
                pe.wait_ge(*ft_c(i, u + 1))
                for t in range(j + 1):
                    last = pe.matmul(f2[h, j * P:(j + 1) * P], fvn[:, t, h], probT[:, t], start=(t == 0), stop=(t == j))
                last.then_inc(fo_mm.sem, 1)
                if u == 7:
                    pass

            pe0 = {"gdn_norm": gdn_norm, "fox_norm": fox_norm, "gdn_gram": gdn_gram, "inv0": inv0, "inv_a": inv_pa,
                   "inv_b": inv_pb, "uw": uw, "scan_v": scan_v, "scan_s": scan_s, "gdn_out": gdn_out,
                   "fox_s": fox_s, "fox_t": fox_t, "fox_o": fox_o}

            def end0(i):
                pe.wait_ge(*go_mm(i))
                pe.wait_ge(*fo_mm(i))
                pe.sem_inc(pe_mix0.sem, 1)

            pe.sem_inc(pe_mix0.sem, 1)
            project0(0)
            pe.wait_ge(*row_v(0, 7))
            pe.wait_ge(*row_a(0, 5))
            for n, (b, r) in enumerate(((g1, row[0]), (g2, row[1]))):
                for t in range(TT):
                    last = pe.transpose(b[:, t * ROWS:(t + 1) * ROWS], r[:, t * P:(t + 1) * P], ident[0:ROWS, 0:ROWS])
                last.then_inc(row_tr.sem, 1)
            with pe.Fori(0, GDN_HEADS - 1) as i:
                project0(i + 1, i)
                end0(i)
            for s in range(L0_SLICES):
                for step, *arg in MIX0[s]:
                    if step in pe0:
                        pe0[step](GDN_HEADS - 1, *arg)
            end0(GDN_HEADS - 1)

            def dense_layer(layer, ph_o, ph_m):
                mix_lo = ((go_lo, fo_lo), (hn_lo, hn_lo))[layer]
                for s in mix_lo:
                    pe.wait_ge(*s((GDN_HEADS, HG_HEADS)[layer] - 1))
                for j in range(KB):
                    for k in range(KB):
                        products(pe, ph_o, 0, j, k, a_hi, a_lo, None)
                stat(1 + 2 * layer)

                def quarter(q):
                    for j in range(KB):
                        for k in range(KB):
                            ready = (lambda k: h_lo_s(1 + 2 * layer, k + 1)) if j == 0 else None
                            products(pe, ph_m, q, j, k, h_hi, h_lo, ready)
                    for j in range(KB):
                        for k in range(KB):
                            ready = (lambda k: alo_s[layer](q, k + 1)) if j == 0 else None
                            products(pe, ph_m, q, KB + j, k, a_hi, a_lo, ready)

                with pe.Fori(0, QUARTERS - 1) as q:
                    quarter(q)
                quarter(QUARTERS - 1)

            dense_layer(0, PH_OUT0, PH_MLP0)
            stat(2)

            def project1(p, mix=None):
                for s in range(L1_SLICES):
                    ready = (lambda k: h_lo_s(2, k + 1)) if isinstance(p, int) and s < KB else None
                    products(pe, PH_L1, p, s // KB, s % KB, h_hi, h_lo, ready)
                    if mix is not None:
                        for step, *arg in MIX1[s]:
                            if step in pe1:
                                pe1[step](mix, *arg)

            def hg_gates(i):
                pe.wait_ge(*act_mix1(i, 1))
                pe.wait_ge(*dve_mix1(i, 1))
                pe.wait_ge(*z1_s[2](i))
                for t in range(TT):
                    last = pe.transpose(g0[:, t * P:(t + 1) * P], z1[2][:, t * P:(t + 1) * P], ident)
                last.then_inc(hv_tr.sem, 1)

            def hg_diag(i):
                pe.wait_ge(*hq_s(i))
                pe.wait_ge(*hk_s(i))
                for t in range(TT):
                    c = slice(t * P, (t + 1) * P)
                    last = pe.matmul(g1[:, c], hk[:, c], hq[:, c], start=True, stop=True)
                last.then_inc(hdg_mm.sem, 1)

            def hg_level(i, l):
                b = (f0, f1)[l % 2]
                pe.wait_ge(*hl_x(i, 2 * l + 2))
                if l >= 2:
                    pe.wait_ge(*hl_c(i, l - 1))
                for t in range(TT):
                    c = slice(t * P, (t + 1) * P)
                    last = pe.matmul(b[:, c], hx[l % 2][:, c], hx[l % 2][:, c], start=True, stop=True)
                last.then_inc(hl_mm.sem, 1)

            def hg_kv(i):
                pe.wait_ge(*hkd_s(i))
                pe.wait_ge(*hv_s(i))
                for t in range(TT):
                    last = pe.transpose(g0[:, t * P:(t + 1) * P], hkd[:, t * P:(t + 1) * P], ident)
                last.then_inc(hkn_tr.sem, 1)
                pe.wait_ge(*hkn_s(i))
                pe.wait_ge(*hdg_s(i))
                for h, b in enumerate((g1, g2)):
                    r = h * CHUNK
                    for c in range(TT):
                        last = pe.matmul(b[:, c * P:(c + 1) * P], hkn[r:r + CHUNK, c], hv[r:r + CHUNK, c],
                                         start=True, stop=True)
                    last.then_inc(hkv_mm.sem, 1)

            def hg_o(i):
                pe.wait_ge(*hl_c(i))
                pe.wait_ge(*hqd_s(i))
                for t in range(TT):
                    pe.matmul(f2[:, t * P:(t + 1) * P], hv[:, t], hA[:, t], start=True, stop=False,
                              skip_group_check=True)
                    for n in (2 * t, 2 * t + 1):
                        c = slice(n * CHUNK, (n + 1) * CHUNK)
                        if n:
                            pe.wait_ge(*hS_s(i, n))
                            last = pe.matmul(f2[:, c], hS[:, n], hqd[:, c], start=False, stop=True,
                                             skip_group_check=True)
                last.then_inc(ho_mm.sem, 1)

            def hg_norm(i):
                pe.wait_ge(*ho_sq(i))
                pe.matmul(g0[:, :], cc("ones"), ho[:, :], start=True, stop=True).then_inc(hn_mm.sem, 1)

            pe1 = {"hg_gates": hg_gates, "hg_diag": hg_diag, "hg_level": hg_level, "hg_kv": hg_kv, "hg_o": hg_o,
                   "hg_norm": hg_norm}

            project1(0)
            with pe.Fori(0, HG_HEADS - 1) as i:
                project1(i + 1, i)
                pe.wait_ge(*hn_mm(i))
                pe.sem_inc(pe_mix1.sem, 1)
            for s in range(L1_SLICES):
                for step, *arg in MIX1[s]:
                    if step in pe1:
                        pe1[step](HG_HEADS - 1, *arg)
            dense_layer(1, PH_OUT1, PH_MLP1)
            for d in range(KB):
                pe.wait_ge(*resid[1](QUARTERS - 1, d + 1))
                if d >= 2:
                    pe.wait_ge(*y_ev(0, d - 1))
                for t in range(TT):
                    last = pe.transpose(mb[d % 2][:, t * P:(t + 1) * P], xT[:, d, t * P:(t + 1) * P], ident)
                last.then_inc(y_tr.sem, 1)

        @block.scalar
        def _(act):
            act.preload_act_table_set(EXP_LN)
            act.wait_ge(const_in.sem, 16)
            act.activation(ident_b[:, :], cc("ident"), ACT.Copy).then_inc(b_const.sem, 1)
            act.activation(neg_b[:, :], cc("fox_neg"), ACT.Copy).then_inc(b_const.sem, 1)
            act.wait_ge(par_in.sem, 32)
            act.wait_ge(wsm_in.sem, 48)
            act.activation(wsm_hi[:, :, :], wsm[:, :, :], ACT.Copy).then_inc(wsm_hi_s.sem, 1)

            def prepare_tile(use, d, ready):
                act.wait_ge(*ready)
                act.activation(h_hi[:, d], xT[:, d], ACT.Copy, scale=pp(gain(use), d)).then_inc(h_hi_s.sem, 1)
                if d >= 2:
                    act.wait_ge(*ssq_s(use, d - 1))
                act.activation(sq[d % 2][:, :], xT[:, d], ACT.Square).then_inc(h_sq.sem, 1)

            def norm(use):
                act.wait_ge(*stat_mm(use))
                act.activation(rstd[:, :], g0[:, :], ACT.Ln, scale=1.0 / D, bias=pp("eps")).then_inc(stat_ln.sem, 1)
                act.wait_ge(*stat_ln(use))
                act.activation(rstd[:, :], rstd[:, :], ACT.Exp, scale=-0.5).then_inc(rstd_s.sem, 1)

            for d in range(KB):
                prepare_tile(0, d, x_ev(0, d + 1))
            norm(0)
            for j in range(LEAD):
                split_hi(act, PH_L0, 0, j)
            r0, r1, r2, r3 = [r[:, :] for r in row]
            act.wait_ge(*row_v(0, 2))
            act.activation(r1, r0, ACT.Abs).then_inc(row_a.sem, 1)
            act.wait_ge(*row_a(0, 1))
            act.activation(r1, r1, ACT.Exp, scale=-1.0).then_inc(row_a.sem, 1)
            act.wait_ge(*row_a(0, 2))
            act.activation(r1, r1, ACT.Ln, bias=cc("ones")[0:ROWS, 0:1]).then_inc(row_a.sem, 1)
            act.activation(small[0:ROWS, 0:1], pp("row_a")[0:ROWS], ACT.Exp).then_inc(row_a.sem, 1)
            act.wait_ge(*row_v(0, 6))
            act.activation(r0[R_B:R_B + GDN_HEADS, :], r2[R_B:R_B + GDN_HEADS, :], ACT.Exp, scale=-1.0)\
                .then_inc(row_a.sem, 1)

            def project0(p, mix=None):
                for j in range(7):
                    if mix is not None:
                        for s in range(j * KB, (j + 1) * KB):
                            for step, *arg in MIX0[s]:
                                if step in act0:
                                    act0[step](mix, *arg)
                    split_hi(act, PH_L0, p, j + LEAD)

            def conv(i):
                for s in (pe_mix0, dve_mix0, pool_mix0):
                    act.wait_ge(*s(i, 1))
                if isinstance(i, int) is False or i == 0:
                    pass
                act.wait_ge(spilled.sem, 16)
                for n in range(2):
                    act.wait_ge(*z0_s[3 + n](i))
                    act.activation(prob[n][:, :], z0[3 + n][:, :], ACT.Square).then_inc(fsq.sem, 1)
                act.wait_ge(*z0_s[6](i))
                act.activation(gate[:, :], z0[6][:, :], ACT.Silu).then_inc(silu_s.sem, 1)
                for n in range(3):
                    act.wait_ge(*conv_s(i, 10 + n))
                    act.activation(cqkv[n][:, :], cqkv[n][:, :], ACT.Silu).then_inc(silu_s.sem, 1)
                act.preload_act_table_set(EXP_LN)
                for n, b in ((0, xm[:, :]), (1, ym[:, :, :].rearrange("p t c -> p (t c)"))):
                    act.wait_ge(*silu_s(i, 2 + n))
                    act.activation(b, cqkv[n][:, :], ACT.Square).then_inc(gsq.sem, 1)

            def rsqrt(i, bank_, buf, mm, k, ln, r, scale):
                act.wait_ge(*mm(i, k))
                act.activation(buf, bank_[:, :], ACT.Ln, scale=scale, bias=pp("eps")).then_inc(ln.sem, 1)
                act.wait_ge(*ln(i, k))
                act.activation(buf, buf, ACT.Exp, scale=-0.5).then_inc(r.sem, 1)

            def fox_norm(i):
                for n, b in ((0, f0), (1, f1)):
                    rsqrt(i, b, prob[n][:, :], fn_mm, n + 1, fn_ln, fn_r, 1.0 / FOX_DH)
                act.wait_ge(*fv_tr(i))
                act.activation(fvn[:, :, :], t4(f2), ACT.Copy).then_inc(fv_ev.sem, 1)

            def gdn_norm(i):
                for n, b in ((0, g0), (1, g1)):
                    buf = (xm[:, :], ym[:, :, :].rearrange("p t c -> p (t c)"))[n]
                    rsqrt(i, b, buf, gn_mm, n + 1, gn_ln, gn_r, 1.0)

            def gdn_gate(i):
                act.wait_ge(*darg_s(i))
                act.activation(dmat[:, :, :], dmat[:, :, :], ACT.Exp).then_inc(dexp_s.sem, 1)
                act.activation(g_bc[:, :], g_bc[:, :], ACT.Exp).then_inc(eg_s.sem, 1)

            def uw(i):
                act.wait_ge(*u_mm(i))
                act.wait_ge(*x_up(i))
                act.activation(xmv, t4(g0), ACT.Copy).then_inc(u_ev.sem, 1)

            def gdn_out(i):
                act.wait_ge(*so_mm(i))
                act.wait_ge(*vnew(i))
                act.activation(xm[:, :], g2[:, :], ACT.Square).then_inc(go_sq.sem, 1)
                rsqrt(i, g0, ym[:, :, :].rearrange("p t c -> p (t c)"), go_mm, 1, go_ln, go_r, 1.0 / DH)
                act.wait_ge(*go_g(i))
                act.activation(a_hi[:, bass.ds(i + FOX_W // P, 1)].rearrange("p o t -> p (o t)"),
                               dstr[:, :, :].rearrange("p t c -> p (t c)"), ACT.Copy).then_inc(go_hi.sem, 1)

            def fox_s(i, u):
                n = (u % TT + 1) * P
                act.wait_ge(*fs_nm(i, u + 1))
                act.activation(prob[u % 2][:, 0:n], prob[u % 2][:, 0:n], ACT.Exp, bias=small[:, 4 + u % 2:5 + u % 2],
                               accum_out=small[:, 6 + u % 2:7 + u % 2]).then_inc(fs_e.sem, 1)

            def fox_t(i, u):
                n = (u % TT + 1) * P
                act.wait_ge(*ft_mm(i, u + 1))
                if u:
                    act.wait_ge(*fo_mm(i, u))
                act.activation(probT[:, 0:u % TT + 1], f1[:, 0:n].rearrange("p (t c) -> p t c", c=P), ACT.Copy)\
                    .then_inc(ft_c.sem, 1)

            def fox_out(i):
                act.wait_ge(*fo_mm(i))
                act.activation(a_hi[:, bass.ds(i, 1)].rearrange("p o t -> p (o t)"), f2[:, :], ACT.Copy)\
                    .then_inc(fo_hi.sem, 1)

            act0 = {"conv": conv, "fox_norm": fox_norm, "gdn_norm": gdn_norm, "gdn_gate": gdn_gate, "uw": uw,
                    "gdn_out": gdn_out, "fox_s": fox_s, "fox_t": fox_t, "fox_out": fox_out}

            def end0(i):
                act.wait_ge(*go_hi(i))
                act.wait_ge(*fo_hi(i))
                act.sem_inc(act_mix0.sem, 1)

            act.sem_inc(act_mix0.sem, 1)
            project0(0)
            act.wait_ge(*row_tr(0, 1))
            act.activation(nat[:, :, :], g1[:, 0:TT * ROWS].rearrange("p (t r) -> p t r", r=ROWS), ACT.Copy)\
                .then_inc(row_a.sem, 1)
            act.wait_ge(*row_tr(0, 2))
            gd = g2[:, 0:TT * ROWS].rearrange("p (t r) -> p t r", r=ROWS)
            act.activation(kd_scale[:, :, :], gd[:, :, R_A:R_A + GDN_HEADS], ACT.Exp).then_inc(row_a.sem, 1)
            act.wait_ge(*row_a(0, 6))
            act.activation(kb_scale[:, :, :], nat[:, :, R_A:R_A + GDN_HEADS], ACT.Exp).then_inc(row_a.sem, 1)
            with act.Fori(0, GDN_HEADS - 1) as i:
                project0(i + 1, i)
                end0(i)
            for s in range(L0_SLICES):
                for step, *arg in MIX0[s]:
                    if step in act0:
                        act0[step](GDN_HEADS - 1, *arg)
            end0(GDN_HEADS - 1)

            def dense_layer(layer, ph_o, ph_m):
                for j in range(KB):
                    split_hi(act, ph_o if j + LEAD < KB else ph_m, 0, (j + LEAD) % KB)
                    prepare_tile(1 + 2 * layer, j, x_out[layer](0, j + 1))
                norm(1 + 2 * layer)

                def quarter(q, last=False):
                    for j in range(2 * KB):
                        if not (last and layer == 1 and j + LEAD >= 2 * KB):
                            split_hi(act, ph_m, q, j + LEAD)
                        if j < KB:
                            act.wait_ge(*relu_s[layer](q, j + 1))
                            if j >= 2:
                                act.wait_ge(*alo_s[layer](q, j - 1))
                            act.activation(act2[j % 2][:, :], relu[j % 2][:, :], ACT.Square).then_inc(sq_s[layer].sem, 1)
                            act.activation(a_hi[:, j], relu[j % 2][:, :], ACT.Square).then_inc(ahi_s[layer].sem, 1)
                        elif last and layer == 0:
                            prepare_tile(2, j - KB, resid[0](QUARTERS - 1, j - KB + 1))

                with act.Fori(0, QUARTERS - 1) as q:
                    quarter(q)
                quarter(QUARTERS - 1, True)

            dense_layer(0, PH_OUT0, PH_MLP0)
            norm(2)
            act.wait_ge(*lb_v(0, 3))
            act.activation(lbs[:, 0], lbs[:, 0], ACT.Exp).then_inc(lb_a.sem, 1)
            act.activation(lbs[:, 1], lbs[:, 1], ACT.Exp).then_inc(lb_a.sem, 1)

            def project1(p, mix=None):
                for j in range(4):
                    split_hi(act, PH_L1, p, j + LEAD)
                    if mix is not None:
                        for s in range(j * KB, (j + 1) * KB):
                            for step, *arg in MIX1[s]:
                                if step in act1:
                                    act1[step](mix, *arg)

            def hg_gates(i):
                for s in (pe_mix1, dve_mix1, pool_mix1):
                    act.wait_ge(*s(i, 1))
                act.wait_ge(*z1_s[0](i))
                act.activation(hq[:, :], z1[0][:, :], ACT.Silu).then_inc(hq_s.sem, 1)
                act.wait_ge(*z1_s[3](i))
                act.activation(hg[:, :], z1[3][:, :], ACT.Silu).then_inc(hg_s.sem, 1)
                act.preload_act_table_set(EXP_LN)
                act.wait_ge(*z1_s[1](i))
                act.activation(hf[:, :], z1[1][:, :], ACT.Exp, scale=-1.0).then_inc(hexp_s.sem, 1)
                act.wait_ge(*hv_tr(i))
                act.activation(hv[:, :, :], t4(g0), ACT.Copy).then_inc(hv_s.sem, 1)
                act.wait_ge(*hf_s(i))
                act.activation(hb[:, :], hf[:, :], ACT.Ln).then_inc(hln_s.sem, 1)

            def hg_diag(i):
                act.wait_ge(*hb_s(i))
                act.activation(hdec[:, :], hf[:, :], ACT.Exp).then_inc(heb_s.sem, 1)
                act.wait_ge(*hka_s(i))
                act.activation(hkd[:, :], hkd[:, :], ACT.Exp).then_inc(hke_s.sem, 1)

            def hg_level(i, l):
                act.wait_ge(*hl_d(i, 2 * l + 2))
                act.activation(he[l % 2][:, :], he[l % 2][:, :], ACT.Exp).then_inc(hl_e.sem, 1)

            def hg_kv(i):
                act.wait_ge(*hkn_tr(i))
                act.activation(hkn[:, :, :], t4(g0), ACT.Copy).then_inc(hkn_s.sem, 1)

            def hg_norm(i):
                act.wait_ge(*ho_mm(i))
                act.wait_ge(*hl_x(i))
                act.activation(ho[:, :], f2[:, :], ACT.Square).then_inc(ho_sq.sem, 1)
                act.wait_ge(*hn_mm(i))
                act.activation(ho[:, :], g0[:, :], ACT.Ln, scale=1.0 / DH, bias=pp("eps")).then_inc(hn_ln.sem, 1)
                act.wait_ge(*hn_ln(i))
                act.activation(ho[:, :], ho[:, :], ACT.Exp, scale=-0.5).then_inc(hn_r.sem, 1)
                act.wait_ge(*hn_g(i))
                act.activation(a_hi[:, bass.ds(i, 1)].rearrange("p o t -> p (o t)"), he[1][:, :], ACT.Copy)\
                    .then_inc(hn_hi.sem, 1)

            act1 = {"hg_gates": hg_gates, "hg_diag": hg_diag, "hg_level": hg_level, "hg_kv": hg_kv,
                    "hg_norm": hg_norm}

            project1(0)
            with act.Fori(0, HG_HEADS - 1) as i:
                project1(i + 1, i)
                act.wait_ge(*hn_hi(i))
                act.sem_inc(act_mix1.sem, 1)
            for s in range(L1_SLICES):
                for step, *arg in MIX1[s]:
                    if step in act1:
                        act1[step](HG_HEADS - 1, *arg)
            dense_layer(1, PH_OUT1, PH_MLP1)

        @block.vector
        def _(dve):
            for k in range(KB):
                dve.wait_ge(*xtr(0, k + 1))
                dve.tensor_copy(xT[:, k], mb[k % 2][:, :]).then_inc(x_ev.sem, 1)

            for n in range(3):
                dve.memset(z0[n][:, 0:3], 0.0).then_inc(pads.sem, 1)

            def rest(use, d):
                dve.wait_ge(*h_hi_s(use, d + 1))
                dve.scalar_tensor_tensor(h_lo[:, d], xT[:, d], pp(gain(use), d), h_hi[:, d].bitcast(F32),
                                         ALU.mult, ALU.subtract).then_inc(h_lo_s.sem, 1)

            for d in range(KB):
                rest(0, d)
            dve.wait_ge(*wsm_hi_s(0))
            dve.tensor_tensor(wsm_lo[:, :, :], wsm[:, :, :], wsm_hi[:, :, :].bitcast(F32), ALU.subtract)\
                .then_inc(wsm_lo_s.sem, 1)
            for j in range(LEAD):
                split_lo(dve, PH_L0, 0, j)
            r0, r1, r2, r3 = [r[:, :] for r in row]
            rp = slice(0, ROWS)
            dve.wait_ge(*row_mm(0))
            dve.wait_ge(*rstd_s(0))
            dve.tensor_tensor(r0, g1[rp, :], rstd[rp, :], ALU.mult).then_inc(row_v.sem, 1)
            dve.wait_ge(*row_v(0, 1))
            dve.tensor_scalar(r0, r0, pp("row_bias")[rp], pp("row_sign")[rp], ALU.add, ALU.mult).then_inc(row_v.sem, 1)
            dve.wait_ge(*row_a(0, 3))
            dve.scalar_tensor_tensor(r2, r0, 0.0, r1, ALU.max, ALU.add).then_inc(row_v.sem, 1)
            dve.wait_ge(*row_a(0, 4))
            dve.tensor_scalar(small[rp, 1:2], small[rp, 0:1], -1.0, None, ALU.mult).then_inc(row_v.sem, 1)
            dve.wait_ge(*row_v(0, 4))
            dve.tensor_scalar(r3, r2, small[rp, 1:2], None, ALU.mult).then_inc(row_v.sem, 1)
            dve.wait_ge(*row_v(0, 5))
            dve.tensor_tensor_scan(r0, row_reset[rp, :], r3, 0.0, ALU.mult, ALU.add).then_inc(row_v.sem, 1)
            dve.wait_ge(*row_v(0, 6))
            r0c = r0.rearrange("p (c t) -> p c t", t=CHUNK)
            dve.wait_ge(*row_a(0, 5))
            dve.tensor_tensor(r1.rearrange("p (c t) -> p c t", t=CHUNK),
                              r0c[:, :, CHUNK - 1:CHUNK].to_broadcast([ROWS, NCH, CHUNK]), r0c, ALU.subtract)\
                .then_inc(row_v.sem, 1)

            def evac0(p, j):
                b = dense[j % 2]
                dve.wait_ge(gemm_done.sem, PH_L0.n(p, j) + 1)
                if not isinstance(p, int):
                    if j < 3:
                        dve.wait_ge(*conv_s(p - 1, 10 + j))
                    elif j < 5:
                        dve.wait_ge(*fn(p - 1, j - 2))
                    elif j == 5:
                        dve.wait_ge(*fv_tr(p - 1))
                    else:
                        dve.wait_ge(*silu_s(p - 1, 1))
                dst = z0[j][:, 3:3 + T] if j < 3 else z0[j][:, :]
                dve.tensor_tensor(dst, b[:, :], rstd[:, :], ALU.mult).then_inc(z0_s[j].sem, 1)

            def project0(p, mix=None):
                for j in range(7):
                    if mix is not None:
                        for s in range(j * KB, (j + 1) * KB):
                            for step, *arg in MIX0[s]:
                                if step in dve0:
                                    dve0[step](mix, *arg)
                    evac0(p, j)
                    dve.wait_ge(*z0_s[j](p))
                    dve.sem_inc(evac_done.sem, 1)
                    split_lo(dve, PH_L0, p, j + LEAD)

            def conv(i):
                for s in (pe_mix0, act_mix0, pool_mix0):
                    dve.wait_ge(*s(i, 1))
                dve.wait_ge(spilled.sem, 16)
                a, _ = _p["conv"]
                for tap in range(3, -1, -1):
                    for n in range(3):
                        w = par[:, bass.ds(i + (a + (tap * 3 + n) * GDN_HEADS), 1)]
                        if tap == 3:
                            dve.wait_ge(*z0_s[n](i))
                            dve.tensor_scalar(cqkv[n][:, :], z0[n][:, 3:3 + T], w, None, ALU.mult)\
                                .then_inc(conv_s.sem, 1)
                        else:
                            dve.wait_ge(*conv_s(i, 3 * (2 - tap) + n + 1))
                            dve.scalar_tensor_tensor(cqkv[n][:, :], z0[n][:, tap:tap + T], w, cqkv[n][:, :],
                                                     ALU.mult, ALU.add).then_inc(conv_s.sem, 1)

            def fox_norm(i):
                for n, (z, o, g) in enumerate(((z0[3], fqn, small[:, 2:3]), (z0[4], fkn, pp("fkn")))):
                    dve.wait_ge(*fn_r(i, n + 1))
                    dve.scalar_tensor_tensor(o[:, :], z[:, :], g, prob[n][:, :], ALU.mult, ALU.mult)\
                        .then_inc(fn.sem, 1)

            def gdn_norm(i):
                dve.wait_ge(*gn_r(i, 1))
                dve.scalar_tensor_tensor(cqkv[0][:, :], cqkv[0][:, :], float(DH) ** -0.5, xm[:, :], ALU.mult, ALU.mult)\
                    .then_inc(gn.sem, 1)
                dve.wait_ge(*gn_r(i, 2))
                dve.tensor_tensor(cqkv[1][:, :], cqkv[1][:, :], ym[:, :, :].rearrange("p t c -> p (t c)"), ALU.mult)\
                    .then_inc(gn.sem, 1)

            def gdn_gate(i):
                dve.wait_ge(g_in.sem, i * 16 + 16)
                for t in range(TT):
                    dve.scalar_tensor_tensor(dmat[:, t], g_bc[:, t * P:(t + 1) * P],
                                             nat[:, t, bass.ds(i + R_A, 1)], cc("causal_neg"),
                                             ALU.subtract, ALU.add).then_inc(darg_s.sem, 1)
                dve.wait_ge(b_in.sem, i * 16 + 16)
                dve.wait_ge(*gn(i))
                dve.tensor_tensor(kbeta[:, :], cqkv[1][:, :], b_bc[:, :], ALU.mult).then_inc(kbeta_s.sem, 1)
                dve.wait_ge(*eg_s(i))
                dve.tensor_tensor(qd[:, :], cqkv[0][:, :], g_bc[:, :], ALU.mult).then_inc(qd_s.sem, 1)

            def per_frame(a, i, at_=0):
                return a[:, :, bass.ds(i + at_, 1)].to_broadcast([P, TT, P])

            def gdn_gram(i):
                dve.wait_ge(*k_tr(i))
                dve.tensor_tensor(kbg[:, :, :], t4(g2), per_frame(kb_scale, i), ALU.mult).then_inc(k_nat.sem, 1)
                dve.tensor_tensor(kdec[:, :, :], t4(g2), per_frame(kd_scale, i), ALU.mult).then_inc(k_nat.sem, 1)
                dve.wait_ge(*v_tr(i))
                dve.tensor_tensor(vb[:, :, :], t4(g0), per_frame(nat, i, R_B), ALU.mult).then_inc(vb_s.sem, 1)
                dve.wait_ge(*gram(i, 1))
                dve.wait_ge(*dstr_s(i))
                dve.tensor_tensor(nmat[:, :, :], t4(g1), dstr[:, :, :], ALU.mult).then_inc(n_s.sem, 1)
                dve.wait_ge(*gram(i, 2))
                dve.tensor_tensor(qkT[:, :, :], t4(g2), dmat[:, :, :], ALU.mult).then_inc(qkT_s.sem, 1)

            def tiles(name):
                a, w = _c[name]
                return cst[:, a:a + w].rearrange("p (o c) -> p o c", o=1).to_broadcast([P, TT, P])

            def inv0(i):
                dve.wait_ge(*n_s(i))
                dve.wait_ge(*gram(i, 1))
                dve.tensor_tensor(ym[:, :, :], nmat[:, :, :], tiles("up0"), ALU.mult).then_inc(y_0.sem, 1)
                dve.wait_ge(*y_0(i, 1))
                dve.tensor_tensor(ym[:, :, :], tiles("ident"), ym[:, :, :], ALU.subtract).then_inc(y_0.sem, 1)
                dve.wait_ge(*inv_a(i, 1))
                dve.tensor_tensor(xmv, t4(g0), tiles("low0"), ALU.mult).then_inc(x_0.sem, 1)
                dve.wait_ge(*x_0(i, 1))
                dve.tensor_tensor(xmv, tiles("ident"), xmv, ALU.subtract).then_inc(x_0.sem, 1)

            def inv_da(i, l):
                dve.wait_ge(*inv_a(i, l + 1))
                dve.tensor_tensor(pm[:, :, :], t4(g0), tiles(f"low{l}"), ALU.mult).then_inc(inv_p.sem, 1)

            def inv_db(i, l):
                if l < LEVELS - 1:
                    dve.wait_ge(*inv_x(i, l))
                    dve.tensor_tensor(xmv, xmv, t4(g1), ALU.subtract).then_inc(x_up.sem, 1)
                dve.wait_ge(*inv_y(i, l))
                dve.tensor_tensor(ym[:, :, :], ym[:, :, :], t4(g2), ALU.subtract).then_inc(y_up.sem, 1)

            def uw(i):
                dve.wait_ge(*w_mm(i))
                dve.tensor_copy(pm[:, :, :], t4(g1)).then_inc(w_ev.sem, 1)

            vnv = t4(cqkv[2])

            def scan_v(i, n):
                r, t = n % 2 * CHUNK, n // 2
                dve.wait_ge(*sv_mm(i, n))
                dve.tensor_tensor(vnv[r:r + CHUNK, t], xmv[r:r + CHUNK, t], g0[r:r + CHUNK, 0:P], ALU.subtract)\
                    .then_inc(vnew.sem, 1)

            def scan_s(i, n):
                if n == 0:
                    dve.wait_ge(*u_ev(i))
                    dve.wait_ge(*v_tr(i))
                    dve.tensor_copy(vnv[0:CHUNK, 0], xmv[0:CHUNK, 0]).then_inc(vnew.sem, 1)
                    dve.wait_ge(*ss_mm(i, 1))
                    dve.tensor_copy(state[:, :], g1[:, 0:P]).then_inc(s_up.sem, 1)
                elif n < NCH - 1:
                    dve.wait_ge(*ss_mm(i, n + 1))
                    dve.wait_ge(*s_up(i, n))
                    last = (n + 1) * CHUNK - 1
                    dve.scalar_tensor_tensor(state[:, :], state[:, :], g_bc[:, last:last + 1], g1[:, 0:P],
                                             ALU.mult, ALU.add).then_inc(s_up.sem, 1)

            def gdn_out(i):
                dve.wait_ge(*go_r(i))
                dve.scalar_tensor_tensor(pm[:, :, :], t4(g2), pp("gdn_o"), ym[:, :, :], ALU.mult, ALU.mult)\
                    .then_inc(go_n.sem, 1)
                dve.wait_ge(*go_hi(i))
                dve.tensor_tensor(a_lo[:, bass.ds(i + FOX_W // P, 1)].rearrange("p o t -> p (o t)"),
                                  dstr[:, :, :].rearrange("p t c -> p (t c)"),
                                  a_hi[:, bass.ds(i + FOX_W // P, 1)].rearrange("p o t -> p (o t)").bitcast(F32),
                                  ALU.subtract).then_inc(go_lo.sem, 1)

            def fox_s(i, u):
                hh, j = u // TT, u % TT
                n = (j + 1) * P
                dve.wait_ge(*fs_mm(i, u + 1))
                if u == 0:
                    for c in c_in:
                        dve.wait_ge(c.sem, i * 16 + 16)
                    dve.wait_ge(*fn(i))
                if u >= 2:
                    dve.wait_ge(*ft_mm(i, u - 1))
                dve.scalar_tensor_tensor(prob[u % 2][:, 0:n], f0[:, 0:n], nat[:, j, bass.ds(i * 2 + hh, 1)],
                                         c_bc[hh][:, 0:n], ALU.add, ALU.subtract).then_inc(fs_s.sem, 1)
                dve.wait_ge(*fs_s(i, u + 1))
                dve.reduce_max(small[:, 8 + u % 2:9 + u % 2], prob[u % 2][:, 0:n], AX.X).then_inc(fs_m.sem, 1)
                dve.wait_ge(*fs_m(i, u + 1))
                if u >= 2:
                    dve.wait_ge(*fs_e(i, u - 1))
                dve.tensor_scalar(small[:, 4 + u % 2:5 + u % 2], small[:, 8 + u % 2:9 + u % 2], -1.0, None, ALU.mult)\
                    .then_inc(fs_nm.sem, 1)

            def fox_t(i, u):
                dve.wait_ge(*fs_e(i, u + 1))
                if u >= 2:
                    dve.wait_ge(*fs_p(i, u - 1))
                dve.reciprocal(small[:, 10 + u % 2:11 + u % 2], small[:, 6 + u % 2:7 + u % 2]).then_inc(fs_r.sem, 1)

            def fox_out(i):
                dve.wait_ge(*fo_hi(i))
                dve.tensor_tensor(a_lo[:, bass.ds(i, 1)].rearrange("p o t -> p (o t)"), f2[:, :],
                                  a_hi[:, bass.ds(i, 1)].rearrange("p o t -> p (o t)").bitcast(F32), ALU.subtract)\
                    .then_inc(fo_lo.sem, 1)

            dve0 = {"conv": conv, "fox_norm": fox_norm, "gdn_norm": gdn_norm, "gdn_gate": gdn_gate,
                    "gdn_gram": gdn_gram, "inv0": inv0, "inv_a": inv_da, "inv_b": inv_db, "uw": uw,
                    "scan_v": scan_v, "scan_s": scan_s, "gdn_out": gdn_out, "fox_s": fox_s, "fox_t": fox_t,
                    "fox_out": fox_out}

            def end0(i):
                dve.wait_ge(*go_lo(i))
                dve.wait_ge(*fo_lo(i))
                dve.sem_inc(dve_mix0.sem, 1)

            dve.wait_ge(par_in.sem, 32)
            dve.wait_ge(*pads(0))
            dve.tensor_scalar(small[:, 2:3], pp("fqn"), float(FOX_DH) ** -0.5, None, ALU.mult).then_inc(row_v.sem, 1)
            dve.wait_ge(*row_v(0, 8))
            dve.sem_inc(dve_mix0.sem, 1)
            project0(0)
            dve.wait_ge(*row_a(0, 8))
            dve.tensor_tensor(kb_scale[:, :, :], kb_scale[:, :, :], nat[:, :, R_B:R_B + GDN_HEADS], ALU.mult)\
                .then_inc(row_v.sem, 1)
            dve.wait_ge(*row_v(0, 9))
            with dve.Fori(0, GDN_HEADS - 1) as i:
                project0(i + 1, i)
                end0(i)
            for s in range(L0_SLICES):
                for step, *arg in MIX0[s]:
                    if step in dve0:
                        dve0[step](GDN_HEADS - 1, *arg)
            end0(GDN_HEADS - 1)

            def dense_layer(layer, ph_o, ph_m):
                use = 1 + 2 * layer
                for j in range(KB):
                    if layer == 0 and j == 0:
                        dve.wait_ge(reloaded.sem, 16)
                    dve.wait_ge(gemm_done.sem, ph_o.n(0, j) + 1)
                    dve.tensor_tensor(xT[:, j], xT[:, j], dense[j % 2][:, :], ALU.add).then_inc(x_out[layer].sem, 1)
                    dve.wait_ge(*x_out[layer](0, j + 1))
                    dve.sem_inc(evac_done.sem, 1)
                    split_lo(dve, ph_o if j + LEAD < KB else ph_m, 0, (j + LEAD) % KB)
                    rest(use, j)
                dve.wait_ge(*rstd_s(use))

                def quarter(q, last=False):
                    for j in range(2 * KB):
                        b = dense[j % 2]
                        dve.wait_ge(gemm_done.sem, ph_m.n(q, j) + 1)
                        if j < KB:
                            if j >= 2:
                                dve.wait_ge(*ahi_s[layer](q, j - 1))
                            dve.scalar_tensor_tensor(relu[j % 2][:, :], b[:, :], 0.0, rstd[:, :], ALU.max, ALU.mult)\
                                .then_inc(relu_s[layer].sem, 1)
                            dve.wait_ge(*relu_s[layer](q, j + 1))
                            dve.sem_inc(evac_done.sem, 1)
                            split_lo(dve, ph_m, q, j + LEAD)
                            dve.wait_ge(*ahi_s[layer](q, j + 1))
                            dve.tensor_tensor(a_lo[:, j], act2[j % 2][:, :], a_hi[:, j].bitcast(F32), ALU.subtract)\
                                .then_inc(alo_s[layer].sem, 1)
                        else:
                            d = j - KB
                            dve.tensor_tensor(xT[:, d], xT[:, d], b[:, :], ALU.add).then_inc(resid[layer].sem, 1)
                            dve.wait_ge(*resid[layer](q, d + 1))
                            dve.sem_inc(evac_done.sem, 1)
                            if not (last and layer == 1 and j + LEAD >= 2 * KB):
                                split_lo(dve, ph_m, q, j + LEAD)
                            if last and layer == 0:
                                rest(2, d)

                with dve.Fori(0, QUARTERS - 1) as q:
                    quarter(q)
                quarter(QUARTERS - 1, True)

            dense_layer(0, PH_OUT0, PH_MLP0)
            l0, l1 = pp("lb0", 0, HG_HEADS), pp("lb1", 0, HG_HEADS)
            dve.tensor_tensor(lbs[:, 2], l0, l1, ALU.max).then_inc(lb_v.sem, 1)
            dve.wait_ge(*lb_v(0, 1))
            dve.tensor_tensor(lbs[:, 0], l0, lbs[:, 2], ALU.subtract).then_inc(lb_v.sem, 1)
            dve.tensor_tensor(lbs[:, 1], l1, lbs[:, 2], ALU.subtract).then_inc(lb_v.sem, 1)
            dve.wait_ge(*lb_a(0))
            dve.tensor_tensor(lbs[:, 2], lbs[:, 0], lbs[:, 1], ALU.add).then_inc(lb_v.sem, 1)
            dve.wait_ge(*lb_v(0, 4))
            dve.reciprocal(lbs[:, 3], lbs[:, 2]).then_inc(lb_v.sem, 1)
            dve.wait_ge(*lb_v(0, 5))
            dve.tensor_tensor(lbs[:, 1], lbs[:, 1], lbs[:, 3], ALU.mult).then_inc(lb_v.sem, 1)
            dve.wait_ge(*lb_v(0, 6))
            dve.tensor_scalar(lbs[:, 2], lbs[:, 1], -1.0, 1.0, ALU.mult, ALU.add).then_inc(lb_v.sem, 1)
            dve.wait_ge(*lb_v(0, 7))
            dve.wait_ge(*rstd_s(2))

            def project1(p, mix=None):
                for j in range(4):
                    if mix is not None:
                        for s in range(j * KB, (j + 1) * KB):
                            for step, *arg in MIX1[s]:
                                if step in dve1:
                                    dve1[step](mix, *arg)
                    dve.wait_ge(gemm_done.sem, PH_L1.n(p, j) + 1)
                    if not isinstance(p, int):
                        dve.wait_ge(*(hq_s, hexp_s, hv_tr, hg_s)[j](p - 1))
                    dve.tensor_tensor(z1[j][:, :], dense[j % 2][:, :], rstd[:, :], ALU.mult).then_inc(z1_s[j].sem, 1)
                    dve.wait_ge(*z1_s[j](p))
                    dve.sem_inc(evac_done.sem, 1)
                    split_lo(dve, PH_L1, p, j + LEAD)

            def chunks(a, m=CHUNK):
                return a[:, :].rearrange("p (c t) -> p c t", t=m)

            def hg_gates(i):
                for s in (pe_mix1, act_mix1, pool_mix1):
                    dve.wait_ge(*s(i, 1))
                dve.wait_ge(*hexp_s(i))
                dve.tensor_scalar(hdec[:, :], hf[:, :], 1.0, None, ALU.add).then_inc(hd_s.sem, 1)
                dve.wait_ge(*hd_s(i))
                dve.reciprocal(hkd[:, :], hdec[:, :]).then_inc(hr_s.sem, 1)
                dve.wait_ge(*hr_s(i))
                dve.tensor_scalar(hf[:, :], hkd[:, :], lbs[:, 2, bass.ds(i, 1)], lbs[:, 1, bass.ds(i, 1)],
                                  ALU.mult, ALU.add).then_inc(hf_s.sem, 1)
                dve.wait_ge(*hf_s(i))
                dve.tensor_scalar(hk[:, :], hf[:, :], -1.0, 1.0, ALU.mult, ALU.add).then_inc(hk_s.sem, 1)
                dve.wait_ge(*hk_s(i))
                dve.wait_ge(*hln_s(i))
                dve.tensor_tensor_scan(hf[:, :], cc("chunk_reset"), hb[:, :], 0.0, ALU.mult, ALU.add)\
                    .then_inc(hb_s.sem, 1)

            def hg_diag(i):
                dve.wait_ge(*hb_s(i))
                dve.tensor_tensor(chunks(hkd), chunks(hf)[:, :, CHUNK - 1:CHUNK].to_broadcast([P, NCH, CHUNK]),
                                  chunks(hf), ALU.subtract).then_inc(hka_s.sem, 1)
                dve.wait_ge(*heb_s(i))
                dve.tensor_tensor(hqd[:, :], hq[:, :], hdec[:, :], ALU.mult).then_inc(hqd_s.sem, 1)
                dve.wait_ge(*hke_s(i))
                dve.tensor_tensor(hkd[:, :], hkd[:, :], hk[:, :], ALU.mult).then_inc(hkd_s.sem, 1)
                dve.wait_ge(*hdg_mm(i))
                dve.tensor_tensor(hA[:, :, :], t4(g1), tiles("ident"), ALU.mult).then_inc(hdg_s.sem, 1)

            def hg_level(i, l):
                h = 1 << l
                e, xx = chunks(he[l % 2], 2 * h), chunks(hx[l % 2], 2 * h)
                dve.wait_ge(*hl_e(i, l + 1))
                if l >= 2:
                    dve.wait_ge(*hl_mm(i, l - 1))
                dve.tensor_tensor(xx[:, :, 0:h], chunks(hk, 2 * h)[:, :, 0:h], e[:, :, 0:h], ALU.mult).then_inc(hl_x.sem, 1)
                dve.tensor_tensor(xx[:, :, h:], chunks(hq, 2 * h)[:, :, h:], e[:, :, h:], ALU.mult).then_inc(hl_x.sem, 1)
                if l:
                    merge(i, l - 1)

            def merge(i, l):
                dve.wait_ge(const_in.sem, 16)
                dve.wait_ge(*hl_mm(i, l + 1))
                dve.wait_ge(*(hl_c(i, l) if l else hdg_s(i)))
                dve.copy_predicated(hA[:, :, :], tiles(f"up{l}").bitcast(U32), t4((f0, f1)[l % 2]))\
                    .then_inc(hl_c.sem, 1)

            def hg_kv(i):
                merge(i, LEVELS - 1)
                for n in range(1, NCH):
                    b = (g1, g2)[(n - 1) % 2]
                    c = (n - 1) // 2
                    if n <= 2:
                        dve.wait_ge(*hkv_mm(i, n))
                    if n == 1:
                        dve.tensor_copy(hS[:, 1], b[:, 0:P]).then_inc(hS_s.sem, 1)
                    else:
                        dve.wait_ge(*hS_s(i, n - 1))
                        last = n * CHUNK - 1
                        dve.scalar_tensor_tensor(hS[:, n], hS[:, n - 1], hdec[:, last:last + 1],
                                                 b[:, c * P:(c + 1) * P], ALU.mult, ALU.add).then_inc(hS_s.sem, 1)

            def hg_norm(i):
                dve.wait_ge(*hn_r(i))
                dve.scalar_tensor_tensor(hx[0][:, :], f2[:, :], pp("hg_o"), ho[:, :], ALU.mult, ALU.mult)\
                    .then_inc(hn_t.sem, 1)
                dve.wait_ge(*hn_hi(i))
                dve.tensor_tensor(a_lo[:, bass.ds(i, 1)].rearrange("p o t -> p (o t)"), he[1][:, :],
                                  a_hi[:, bass.ds(i, 1)].rearrange("p o t -> p (o t)").bitcast(F32), ALU.subtract)\
                    .then_inc(hn_lo.sem, 1)

            dve1 = {"hg_gates": hg_gates, "hg_diag": hg_diag, "hg_level": hg_level, "hg_kv": hg_kv,
                    "hg_norm": hg_norm}

            project1(0)
            with dve.Fori(0, HG_HEADS - 1) as i:
                project1(i + 1, i)
                dve.wait_ge(*hn_lo(i))
                dve.sem_inc(dve_mix1.sem, 1)
            for s in range(L1_SLICES):
                for step, *arg in MIX1[s]:
                    if step in dve1:
                        dve1[step](HG_HEADS - 1, *arg)
            dense_layer(1, PH_OUT1, PH_MLP1)
            for d in range(KB):
                dve.wait_ge(*y_tr(0, d + 1))
                if d >= 2:
                    dve.wait_ge(stored[d % 2].sem, 16 * (d // 2))
                dve.tensor_copy(yn[:, d % 2], t4(mb[d % 2])).then_inc(y_ev.sem, 1)

        @block.gpsimd
        def _(pool):
            pool.memset(wsm[:, :, :], 0.0).then_inc(wsm_z.sem, 1)

            def sum_squares(use):
                for d in range(KB):
                    pool.wait_ge(*h_sq(use, d + 1))
                    if d == 0:
                        pool.tensor_copy(ssq[:, :], sq[0][:, :]).then_inc(ssq_s.sem, 1)
                    else:
                        pool.wait_ge(*ssq_s(use, d))
                        pool.tensor_tensor(ssq[:, :], ssq[:, :], sq[d % 2][:, :], ALU.add).then_inc(ssq_s.sem, 1)

            sum_squares(0)

            def rows(i):
                for s in (pe_mix0, act_mix0, dve_mix0):
                    pool.wait_ge(*s(i, 1))
                for dst, r, s in ((c_bc[0], i * 2 + R_F, c_in[0]), (c_bc[1], i * 2 + (R_F + 1), c_in[1]),
                                  (g_bc, i + R_A, g_in), (b_bc, i + R_B, b_in)):
                    pool.dma_start(dst[:, :], rows_dram[bass.ds(r, 1), :].partition_broadcast(P)
                                   .rearrange("p o t -> p (o t)")).then_inc(s.sem, 16)

            def gdn_gate(i):
                a, w = _c["strict"]
                pool.wait_ge(*dexp_s(i))
                pool.tensor_tensor(dstr[:, :, :], dmat[:, :, :],
                                   cst[:, a:a + w].rearrange("p (o c) -> p o c", o=1).to_broadcast([P, TT, P]),
                                   ALU.mult).then_inc(dstr_s.sem, 1)

            def fox_t(i, u):
                n = (u % TT + 1) * P
                pool.wait_ge(*fs_r(i, u + 1))
                pool.tensor_tensor(prob[u % 2][:, 0:n], prob[u % 2][:, 0:n],
                                   small[:, 10 + u % 2:11 + u % 2].to_broadcast([P, n]), ALU.mult)\
                    .then_inc(fs_p.sem, 1)

            def gdn_out(i):
                pool.wait_ge(*go_n(i))
                pool.wait_ge(*n_s(i))
                pool.tensor_tensor(dstr[:, :, :].rearrange("p t c -> p (t c)"),
                                   pm[:, :, :].rearrange("p t c -> p (t c)"), gate[:, :], ALU.mult)\
                    .then_inc(go_g.sem, 1)

            pool0 = {"conv": rows, "gdn_gate": gdn_gate, "fox_t": fox_t, "gdn_out": gdn_out}

            def mix0(i):
                for s in range(L0_SLICES):
                    for step, *arg in MIX0[s]:
                        if step in pool0:
                            pool0[step](i, *arg)
                pool.wait_ge(*go_g(i))
                pool.wait_ge(*fs_p(i))
                pool.sem_inc(pool_mix0.sem, 1)

            pool.wait_ge(*ssq_s(0))
            pool.sem_inc(pool_mix0.sem, 1)
            pool.wait_ge(row_out.sem, 16)
            pool.wait_ge(spilled.sem, 16)
            with pool.Fori(0, GDN_HEADS) as i:
                mix0(i)
            sum_squares(1)
            sum_squares(2)

            def hg_level(i, l):
                h = 1 << l
                bb = hf[:, :].rearrange("p (c t) -> p c t", t=2 * h)
                e = he[l % 2][:, :].rearrange("p (c t) -> p c t", t=2 * h)
                ref = bb[:, :, h - 1:h].to_broadcast([P, T // (2 * h), h])
                if l >= 2:
                    pool.wait_ge(*hl_x(i, 2 * l - 2))
                pool.tensor_tensor(e[:, :, 0:h], ref, bb[:, :, 0:h], ALU.subtract).then_inc(hl_d.sem, 1)
                pool.tensor_tensor(e[:, :, h:], bb[:, :, h:], ref, ALU.subtract).then_inc(hl_d.sem, 1)

            def mix1(i):
                for s in (pe_mix1, act_mix1, dve_mix1):
                    pool.wait_ge(*s(i, 1))
                pool.wait_ge(*hb_s(i))
                for l in range(LEVELS):
                    hg_level(i, l)
                pool.wait_ge(*hn_t(i))
                pool.tensor_tensor(he[1][:, :], hx[0][:, :], hg[:, :], ALU.mult).then_inc(hn_g.sem, 1)
                pool.wait_ge(*hn_g(i))
                pool.sem_inc(pool_mix1.sem, 1)

            with pool.Fori(0, HG_HEADS) as i:
                mix1(i)
            sum_squares(3)


def pack_params(a):
    out = np.zeros((P, PARAM_W), np.float32)

    def put(name, v):
        at, w = _p[name]
        out[:v.shape[0], at:at + w] = v

    for n, name in enumerate(("l0_mix_norm", "l0_ffn_norm", "l1_mix_norm", "l1_ffn_norm")):
        put(f"g{n}", a[name].reshape(KB, P).T)
    put("fqn", np.concatenate([a["l0_fox_q_norm"]] * 2)[:, None])
    put("fkn", np.concatenate([a["l0_fox_k_norm"]] * 2)[:, None])
    put("gdn_o", a["l0_gdn_o_norm"][:, None])
    put("hg_o", a["l1_hgrn_o_norm"][:, None])
    put("conv", a["l0_gdn_conv"].reshape(4 * 3 * GDN_HEADS, P).T)
    put("lb0", a["hgrn_lb_logits"][0].reshape(HG_HEADS, P).T)
    put("lb1", a["hgrn_lb_logits"][1].reshape(HG_HEADS, P).T)
    at = _p["row_bias"][0]
    out[R_F:R_F + FOX_HEADS, at] = a["l0_fox_f_bias"]
    out[R_A:R_A + GDN_HEADS, at] = a["l0_gdn_dt_bias"]
    out[R_A:R_A + GDN_HEADS, _p["row_a"][0]] = a["l0_gdn_A_log"]
    out[:, _p["row_sign"][0]] = np.where(np.arange(P) < R_A, -1.0, 1.0)
    out[:, _p["eps"][0]] = EPS
    return out


def kernel(**inputs):
    import concourse.bacc as bacc
    from concourse.bass_utils import run_bass_kernel_spmd

    a = {k: np.ascontiguousarray(v) for k, v in inputs.items()}
    arrays = {n: a[n] for n in ("x", "l0_w_in", "l0_w_out", "l0_w_ff1", "l0_w_ff2", "l1_w_in", "l1_w_out",
                                "l1_w_ff1", "l1_w_ff2")}
    arrays["params"] = pack_params(a)
    arrays["consts"] = constants()
    nc = bacc.Bacc("TRN2", target_bir_lowering=False, num_devices=1)
    aps = [nc.dram_tensor(f"in_{n}", v.shape, F32, kind="ExternalInput").ap() for n, v in arrays.items()]
    out = nc.dram_tensor("y", (1, T, D), F32, kind="ExternalOutput").ap()
    build(nc, *aps, out)
    r = run_bass_kernel_spmd(nc, [{f"in_{n}": v for n, v in arrays.items()}], core_ids=[0])
    return r.results[0]["y"]
```

```python
import concourse.bass as bass
import numpy as np
from concourse import mybir

F32 = mybir.dt.float32
F32R = mybir.dt.float32r
BF16 = mybir.dt.bfloat16
U32 = mybir.dt.uint32
ALU = mybir.AluOpType
ACT = mybir.ActivationFunctionType
AX = mybir.AxisListType

P = 128
T = 512
D = 1024
KB = D // P
TT = T // P
CHUNK = 64
NCH = T // CHUNK
FF = 4 * D
QUARTERS = FF // D
FOX_HEADS, FOX_DH = 8, 64
GDN_HEADS, DH = 4, 128
FOX_W, GDN_W = FOX_HEADS * FOX_DH, GDN_HEADS * DH
HG_HEADS = 8
EPS = 1e-6
NEG = -1.0e30

O_FQ, O_FK, O_FV, O_FF = 0, FOX_W, 2 * FOX_W, 3 * FOX_W
O_GQ = O_FF + FOX_HEADS
O_GK, O_GV = O_GQ + GDN_W, O_GQ + 2 * GDN_W
O_GB = O_GQ + 3 * GDN_W
O_GA = O_GB + GDN_HEADS
O_GG = O_GA + GDN_HEADS
R_F, R_B, R_A, ROWS = 0, 32, 64, 96

LEVELS = 6

_c = {}


def _cols(names):
    at = 0
    for name, width in names:
        _c[name] = (at, width)
        at += width
    return at


CONST_W = _cols([("ident", P), ("causal_neg", P), ("strict", P), ("fox_neg", P), ("ones", P), ("pair_ones", P)]
                + [(f"low{b}", P) for b in range(LEVELS)] + [(f"up{b}", P) for b in range(LEVELS)]
                + [("chunk_reset", T)])
_c["row_reset"] = (CONST_W, T)
_p = {}
_at = 0
for _n, _w in [("g0", KB), ("g1", KB), ("g2", KB), ("g3", KB), ("fqn", 1), ("fkn", 1), ("gdn_o", 1), ("hg_o", 1),
               ("conv", 4 * 3 * GDN_HEADS), ("lb0", HG_HEADS), ("lb1", HG_HEADS), ("row_bias", 1), ("row_a", 1),
               ("row_sign", 1), ("eps", 1)]:
    _p[_n] = (_at, _w)
    _at += _w
PARAM_W = _at


def constants():
    r, c = np.arange(P)[:, None], np.arange(P)[None, :]
    same = r // CHUNK == c // CHUNK
    out = np.zeros((P, CONST_W + T), np.float32)

    def put(name, a):
        at, w = _c[name]
        out[:, at:at + w] = a

    put("ident", r == c)
    put("causal_neg", np.where(same & (c >= r), 0.0, NEG))
    put("strict", same & (c > r))
    put("fox_neg", np.where(c > r, NEG, 0.0))
    put("ones", 1.0)
    put("pair_ones", r // FOX_DH == c // FOX_DH)
    for b in range(LEVELS):
        h = 1 << b
        block = r // (2 * h) == c // (2 * h)
        low = block & (r % (2 * h) >= h) & (c % (2 * h) < h)
        put(f"low{b}", low)
        put(f"up{b}", low.T)
    t = np.arange(T)[None, :]
    put("chunk_reset", (t % CHUNK != 0))
    put("row_reset", np.where(np.arange(P)[:, None] < R_A, 1.0, (t % CHUNK != 0)))
    return out


class Signal:

    def __init__(self, sem, per, first=0):
        self.sem, self.per, self.first = sem, per, first

    def __call__(self, i, k=None):
        return self.sem, i * self.per + (self.first + (self.per if k is None else k))


EXP_LN = "natural_log_exp_and_others"
LEAD = 3
RAW, SPLIT = 8, 4


class Phase:

    def __init__(self, passes, tiles, raw_slots, before):
        self.passes, self.tiles, self.raw_slots = passes, tiles, raw_slots
        self.base = before.base + before.passes * before.tiles if before else 0
        self.uses = list(before.uses_after()) if before else [0] * RAW
        self.before = before

    def uses_after(self):
        return [u + self.passes * sum(1 for j in range(self.tiles) if j % self.raw_slots == s)
                for s, u in enumerate(self.uses)]

    def n(self, p, j):
        return p * self.tiles + (self.base + j)

    def raw(self, j):
        return j % self.tiles % self.raw_slots

    def split(self, j):
        return j % self.tiles % SPLIT

    def arrivals(self, p, j):
        extra, j = divmod(j, self.tiles)
        s = j % self.raw_slots
        per = sum(1 for x in range(self.tiles) if x % self.raw_slots == s)
        return (p + extra) * per + (self.uses[s] + j // self.raw_slots + 1)

    def split_back(self, j):
        j = j % self.tiles
        pat = [self.split(x) for x in range(self.tiles)] * 3
        at = j + 2 * self.tiles
        return next(d for d in range(1, 2 * self.tiles + 1) if pat[at - d] == pat[at])


PH_L0 = Phase(GDN_HEADS, 7, 7, None)
PH_OUT0 = Phase(1, 8, 8, PH_L0)
PH_MLP0 = Phase(QUARTERS, 16, 8, PH_OUT0)
PH_L1 = Phase(HG_HEADS, 4, 4, PH_MLP0)
PH_OUT1 = Phase(1, 8, 8, PH_L1)
PH_MLP1 = Phase(QUARTERS, 16, 8, PH_OUT1)
TILES = PH_MLP1.base + PH_MLP1.passes * PH_MLP1.tiles



def schedule(slots, *chains):
    at = [[] for _ in range(slots)]
    for chain in chains:
        for step, slot in chain:
            at[min(slot, slots - 1)].append(step)
    return at


L0_SLICES = 7 * KB
_gdn = [(("conv_qk",), 0), (("fox_squares",), 0), (("fox_rows",), 0), (("gdn_rms",), 0), (("fox_norm",), 2),
        (("gdn_rows",), 2), (("conv_v",), 3), (("silu",), 3), (("gdn_v",), 9), (("gdn_split",), 9), (("decays",), 10),
        (("gdn_norm",), 11), (("gdn_scaled",), 14), (("gdn_gram",), 16), (("inv0",), 19)]
_slot = 21.0
for _l in range(1, LEVELS):
    _gdn += [(("inv_a", _l), int(_slot)), (("inv_b", _l), int(_slot + 1.5))]
    _slot += 3
_gdn += [(("uw",), int(_slot))]
_slot += 2
for _n in range(NCH):
    if _n:
        _gdn += [(("scan_v", _n), int(_slot))]
        _slot += 1.15
    _gdn += [(("scan_s", _n), int(_slot))]
    _slot += 1.15
_gdn += [(("gdn_out",), 55)]
_fox = []
for _u in range(8):
    if _u >= 2:
        _fox += [(("fox_t", _u - 2), 8 + 5 * _u)]
    _fox += [(("fox_s", _u), 9 + 5 * _u), (("fox_recip", _u), 13 + 5 * _u)]
    if _u >= 2:
        _fox += [(("fox_o", _u - 2), 11 + 5 * _u)]
_fox += [(("fox_t", 6), 48), (("fox_o", 6), 50), (("fox_t", 7), 52), (("fox_o", 7), 54), (("fox_out",), 55)]
MIX0 = schedule(L0_SLICES, _gdn, _fox)

L1_SLICES = 4 * KB
_hg = [(("hg_norm",), 0), (("hg_f",), 0), (("hg_silu",), 1), (("hg_log",), 2), (("hg_v",), 7), (("hg_norm_split",), 10),
       (("hg_diag",), 10), (("hg_kn",), 13), (("hg_diag_own",), 13)]
_hg_exp = [(("hg_exp", _l), 9 + 2 * _l) for _l in range(LEVELS)]
_hg_scale = [(("hg_scale", _l), 10 + 2 * _l) for _l in range(LEVELS)]
_hg_level = [(("hg_level", _l), 14 + 2 * _l) for _l in range(LEVELS)]
_hg_merge = [(("hg_merge", _l), 15 + 2 * _l) for _l in range(LEVELS)]
_hg_state = [(("hg_kv",), 18), (("hg_state",), 20), (("hg_o",), 28), (("hg_square",), 30)]
CONVOLVED = (7, 8, 12)
LATE = {"gdn_rms", "gdn_split", "hg_norm", "hg_norm_split"}
MIX1 = schedule(L1_SLICES, _hg_exp, _hg_scale, _hg, _hg_level, _hg_merge, _hg_state)


def run_steps(steps, mine, i):
    for step, *arg in steps:
        if step in mine:
            if step not in LATE:
                mine[step](i, *arg)
            elif not (isinstance(i, int) and i == 0):
                mine[step](i - 1, *arg)



def build(nc, x, w_in0, w_out0, w_ff1_0, w_ff2_0, w_in1, w_out1, w_ff1_1, w_ff2_1, params, consts, out):
    spill = nc.dram_tensor("residual_spill", (P, KB * T), F32).ap()
    rows_dram = nc.dram_tensor("gate_rows", (ROWS, T), F32).ap()

    at = [(nc.sbuf_base + 31) // 32 * 32]

    def place(name, shape, dtype, here=None):
        size = (4 if dtype != BF16 else 2) * int(np.prod(shape[1:]))
        size = (size + 31) // 32 * 32
        spot = at if here is None else here
        t = nc.alloc_sbuf_tensor_at(name, list(shape), dtype, offset=spot[0])
        spot[0] += size
        return t

    h_hi = place("h_hi", [P, KB, T], F32R)
    h_lo = place("h_lo", [P, KB, T], F32R)
    a_hi = place("a_hi", [P, KB, T], F32R)
    a_lo = place("a_lo", [P, KB, T], F32R)
    raw = place("w_raw", [P, RAW, KB, P], F32)
    w_hi = place("w_hi", [P, SPLIT, KB, P], F32R)
    w_lo = place("w_lo", [P, SPLIT, KB, P], F32R)
    cst = place("consts", [P, CONST_W], F32)
    par = place("params", [P, PARAM_W], F32)
    rstd = place("rstd", [P, T], F32)
    neg_b = place("fox_neg_b", [P, P], BF16)
    ident_b = place("ident_b", [P, P], BF16)
    nat = place("rows_nat", [P, TT, ROWS], F32)
    kb_scale = place("kb_scale", [P, TT, GDN_HEADS], F32)
    kd_scale = place("kd_scale", [P, TT, GDN_HEADS], F32)
    small = place("small", [P, 16], F32)
    lbs = place("lower_bound", [P, 4, HG_HEADS], F32)

    xt_at = at[0]
    xT = place("xT", [P, KB, T], F32)
    mix_at = at[0]

    def cc(name):
        a, w = _c[name]
        return cst[:, a:a + w]

    def pp(name, k=0, n=1):
        a, _ = _p[name]
        return par[:, a + k:a + k + n]

    m = [mix_at]
    xn = place("x_nat", [P, TT, D], F32, m)
    wsm = place("w_small", [P, KB, ROWS], F32, m)
    wsm_hi = place("w_small_hi", [P, KB, ROWS], F32R, m)
    wsm_lo = place("w_small_lo", [P, KB, ROWS], F32R, m)
    row = [place(f"row{i}", [ROWS, T], F32, m) for i in range(4)]
    row_reset = place("row_reset", [P, T], F32, m)
    assert m[0] <= mix_at + 38 * 1024
    m = [mix_at + 38 * 1024]
    sq = [place(f"sq{i}", [P, T], F32, m) for i in range(2)]
    ssq = place("ssq", [P, T], F32, m)
    m = [mix_at]
    relu = [place(f"relu{i}", [P, T], F32, m) for i in range(2)]
    act2 = [place(f"act2_{i}", [P, T], F32, m) for i in range(2)]
    yn = place("y_nat", [P, 2, TT, P], F32, m)
    m = [xt_at]
    cqkv = [place(f"conv_{s}", [P, T], F32, m) for s in "qkv"]
    g_bc = place("g_bc", [P, T], F32, m)
    b_bc = place("beta_bc", [P, T], F32, m)
    c_bc = [place(f"c_bc{i}", [P, T], F32, m) for i in range(2)]
    qd = place("q_dec", [P, T], F32, m)
    assert m[0] <= mix_at
    m[0] = mix_at
    z0 = [place(f"z_{s}", [P, 3 + T] if s[0] == "g" and s != "gg" else [P, T], F32, m)
          for s in ("gq", "gk", "gv", "fq", "fk", "fv", "gg")]
    assert m[0] <= mix_at + TT * D * 4
    kbeta = place("k_beta", [P, T], F32, m)
    dmat = place("decay", [P, TT, P], F32, m)
    vb = place("v_beta", [P, TT, P], F32, m)
    kbg = place("kb_g", [P, TT, P], F32, m)
    kdec = place("k_dec", [P, TT, P], F32, m)
    nmat = place("n_mat", [P, TT, P], F32, m)
    qkT = place("qkT", [P, TT, P], F32, m)
    gate = place("gate", [P, T], F32, m)
    fqn = place("fqn", [P, T], F32, m)
    fkn = place("fkn", [P, T], F32, m)
    fvn = place("fv_nat", [P, TT, P], F32, m)
    prob = [place(f"prob{i}", [P, T], F32, m) for i in range(2)]
    probT = place("probT", [P, TT, P], F32, m)
    state = place("state", [P, P], F32, m)
    xm = kbeta
    ym = place("inv_t", [P, TT, P], F32, m)
    pm = place("inv_p", [P, TT, P], F32, m)
    dstr = pm
    xmv = xm[:, :].rearrange("p (t c) -> p t c", c=P)
    print("SBUF end of layer 0 mixers:", m[0])
    m = [mix_at]
    z1 = [place(f"z1_{s}", [P, T], F32, m) for s in "qfig"]
    hq = place("h_q", [P, T], F32, m)
    hk = place("h_k", [P, T], F32, m)
    hf = place("h_f", [P, T], F32, m)
    hb = place("h_b", [P, T], F32, m)
    hdec = place("h_dec", [P, T], F32, m)
    hqd = place("h_qd", [P, T], F32, m)
    hkd = place("h_kd", [P, T], F32, m)
    hv = place("h_v", [P, TT, P], F32, m)
    hkn = place("h_kn", [P, TT, P], F32, m)
    he = [place(f"h_e{i}", [P, T], F32, m) for i in range(2)]
    hx = [place(f"h_x{i}", [P, T], F32, m) for i in range(2)]
    hA = place("h_A", [P, TT, P], F32, m)
    hS = place("h_S", [P, NCH, P], F32, m)
    hg = place("h_gate", [P, T], F32, m)
    gain_gate = place("h_gain_gate", [P, T], F32, m)
    hgo = place("h_gated", [P, T], F32, m)
    print("SBUF end of layer 1 mixers:", m[0], "limit", nc.sbuf_usable_end)
    ho = he[0]
    ht = hx[0]

    def bank(name):
        return nc.alloc_psum_tensor(name, [P, T], F32)

    dense = [bank("dense0"), bank("dense1")]
    mb = [bank(f"mix{i}") for i in range(6)]
    g0, g1, g2, f0, f1, f2 = mb

    sems = {}

    def sig(name, per=1, first=0):
        if name not in sems:
            sems[name] = nc.alloc_semaphore(name)
        return Signal(sems[name], per, first)

    def t4(a):
        return a[:, :].rearrange("p (t c) -> p t c", c=P)

    raw_in = [sig(f"raw_in{s}") for s in range(RAW)]
    hi_done = sig("w_hi_done")
    lo_done = sig("w_lo_done")
    gemm_done = sig("gemm_done")
    evac_done = sig("evac_done")
    const_in = sig("const_in")
    x_in = sig("x_in")
    par_in = sig("params_in")
    wsm_z = sig("w_small_zeroed")
    wsm_in = sig("w_small_in")
    xtr = sig("x_transposed", KB)
    x_ev = sig("x_evacuated", KB)
    b_const = sig("bf16_consts", 2)
    h_hi_s = sig("h_hi_ready", KB)
    h_sq = sig("h_squares", KB)
    h_lo_s = sig("h_lo_ready", KB)
    ssq_s = sig("squares_summed", KB)
    stat_mm = sig("stat_mm")
    stat_ln = sig("stat_ln")
    rstd_s = sig("rstd_ready")
    wsm_hi_s, wsm_lo_s = sig("w_small_hi_s"), sig("w_small_lo_s")
    row_mm = sig("row_mm")
    row_v = sig("row_vector", 9)
    row_a = sig("row_scalar", 8)
    row_tr = sig("row_transposed", 2)
    row_out = sig("rows_written")
    spilled = sig("x_spilled")
    reloaded = sig("x_reloaded")
    pads = sig("conv_pads", 3)
    z0_s = [sig(f"projected{i}") for i in range(7)]
    g_in, b_in, c_in = sig("g_bc_in"), sig("beta_bc_in"), [sig("c0_in"), sig("c1_in")]
    conv_s = sig("conv", 12)
    silu_s = sig("silu", 4)
    gsq = sig("gdn_squares", 2)
    fsq = sig("fox_squares", 2)
    gn_mm, gn_ln, gn_r, gn = sig("gdn_norm_mm", 2), sig("gdn_norm_ln", 2), sig("gdn_norm_r", 2), sig("gdn_normed", 2)
    fn_mm, fn_ln, fn_r, fn = sig("fox_norm_mm", 2), sig("fox_norm_ln", 2), sig("fox_norm_r", 2), sig("fox_normed", 2)
    kbeta_s, darg_s, dexp_s, eg_s, qd_s, dstr_s = (sig("k_beta_s"), sig("decay_arg", TT), sig("decay_exp"),
                                                  sig("exp_g"), sig("q_dec_s"), sig("decay_strict_s"))
    k_tr, v_tr, fv_tr, fv_ev = sig("k_tr"), sig("v_tr"), sig("fv_tr"), sig("fv_nat_s")
    k_nat, vb_s = sig("k_nat", 2), sig("vb_s")
    gram, n_s, qkT_s = sig("gram", 2), sig("n_mat_s"), sig("qkT_s")
    inv_a, inv_p, inv_x, inv_y = sig("inv_a", LEVELS), sig("inv_p_s", 5), sig("inv_x", 4), sig("inv_y", 5)
    x_0, y_0, x_up, y_up = sig("x_0", 2), sig("y_0", 2), sig("x_up", 4), sig("y_up", 5)
    u_mm, w_mm, u_ev, w_ev = sig("u_mm"), sig("w_mm"), sig("u_ev"), sig("w_ev")
    sv_mm, vnew, ss_mm, so_mm, s_up = (sig("scan_v_mm", NCH - 1), sig("v_new", NCH), sig("scan_s_mm", NCH - 1),
                                       sig("scan_o_mm", NCH), sig("state_up", NCH - 1))
    go_sq, go_mm, go_ln, go_r, go_n, go_g, go_hi, go_lo = [sig(f"mix_out_{s}") for s in
                                                         ("sq", "mm", "ln", "r", "n", "g", "hi", "lo")]
    fs_mm, fs_s, fs_m, fs_nm, fs_e, fs_r, fs_p = [sig(f"fox_{s}", 8) for s in
                                                  ("s_mm", "s", "max", "negmax", "exp", "recip", "prob")]
    ft_mm, ft_c, fo_mm = sig("fox_t_mm", 8), sig("fox_t_c", 8), sig("fox_o_mm", 8)
    fo_hi, fo_lo = sig("fox_out_hi"), sig("fox_out_lo")
    relu_s, sq_s, ahi_s, alo_s = [[sig(n, KB, l * KB * QUARTERS) for l in range(2)]
                                    for n in ("relu", "relu2", "a_hi", "a_lo")]
    resid = [sig("residual", KB, l * KB * QUARTERS) for l in range(2)]
    x_out = [sig("x_after_mix", KB, l * KB) for l in range(2)]
    z1_s = [sig(f"projected{i}", 1, GDN_HEADS) for i in range(4)]
    lb_a, lb_v = sig("lb_scalar", 2), sig("lb_vector", 8)
    hq_s, hg_s, hexp_s, hd_s, hr_s, hf_s, hk_s, hln_s, hb_s = [sig(f"hg_{s}") for s in
        ("q", "gate", "exp", "den", "rec", "f", "k", "ln", "b")]
    heb_s, hqd_s, hka_s, hke_s, hkd_s = [sig(f"hg_{s}") for s in ("eb", "qd", "karg", "kexp", "kd")]
    hv_tr, hv_s, hkn_tr, hkn_s, hdg_mm, hdg_s = [sig(f"hg_{s}") for s in ("v_tr", "v", "kn_tr", "kn", "diag_mm", "diag")]
    hl_d, hl_e, hl_x, hl_mm, hl_c = (sig("hgl_arg", 12), sig("hgl_exp", 6), sig("hgl_x", 12), sig("hgl_mm", 6),
                                     sig("hgl_copy", 6))
    hkv_mm, hS_s, ho_mm = sig("hg_kv_mm", 2), sig("hg_S", NCH - 1), sig("hg_o_mm")
    ho_sq, hn_mm, hn_ln, hn_r, hn_t, hn_g, hn_hi, hn_lo = [sig(f"mix_out_{s}", 1, GDN_HEADS) for s in
                                                           ("sq", "mm", "ln", "r", "n", "g", "hi", "lo")]
    hgk_s = sig("hg_gain_gate")
    y_tr, y_ev = sig("y_transposed", KB), sig("y_evacuated", KB)
    stored = [sig("stored0"), sig("stored1")]
    print("semaphores:", len(sems))

    def gain(use):
        return f"g{use}"

    def load(sp, ph, p, j, src, back):
        if back is not None:
            sp.wait_ge(lo_done.sem, ph.n(p, j) - (back - 1))
        sp.dma_start(raw[:, ph.raw(j)], src).then_inc(raw_in[ph.raw(j)].sem, 16)

    def split_hi(act, ph, p, j):
        act.wait_ge(raw_in[ph.raw(j)].sem, 16 * ph.arrivals(p, j))
        first = isinstance(p, int) and ph.n(p, j) < SPLIT
        if not first:
            act.wait_ge(gemm_done.sem, ph.n(p, j) - (back_of(ph, j) - 1))
        act.activation(w_hi[:, ph.split(j)], raw[:, ph.raw(j)], ACT.Copy).then_inc(hi_done.sem, 1)

    def back_of(ph, j):
        if ph is PH_OUT0 and j < SPLIT:
            return [3, 3, 3, 7][j]
        return ph.split_back(j)

    def split_lo(dve, ph, p, j):
        dve.wait_ge(hi_done.sem, ph.n(p, j) + 1)
        dve.tensor_tensor(w_lo[:, ph.split(j)], raw[:, ph.raw(j)], w_hi[:, ph.split(j)].bitcast(F32),
                          ALU.subtract).then_inc(lo_done.sem, 1)

    def products(pe, ph, p, j, k, xhi, xlo, ready):
        n, s = ph.n(p, j), ph.split(j)
        if k == 0:
            pe.wait_ge(lo_done.sem, n + 1)
            if not (isinstance(n, int) and n < 2):
                prev = 0 if (ph is PH_L0 and j == 0) else 1
                pe.wait_ge(evac_done.sem, n - prev)
        if ready is not None:
            pe.wait_ge(*ready(k))
        b = dense[j % 2]
        pe.matmul(b[:, :], w_hi[:, s, k], xhi[:, k], start=(k == 0), stop=False)
        pe.matmul(b[:, :], w_lo[:, s, k], xhi[:, k], start=False, stop=False)
        last = pe.matmul(b[:, :], w_hi[:, s, k], xlo[:, k], start=False, stop=(k == KB - 1))
        if k == KB - 1:
            last.then_inc(gemm_done.sem, 1)

    block = nc.Block()
    with block:

        @block.sync
        def _(sp):
            sp.dma_start(xn[:, :, :], x.rearrange("o (t p) d -> p (o t) d", p=P)).then_inc(x_in.sem, 16)
            sp.dma_start(cst[:, :], consts[:, 0:CONST_W]).then_inc(const_in.sem, 16)
            sp.dma_start(par[:, :], params).then_inc(par_in.sem, 16)
            sp.dma_start(row_reset[:, :], consts[:, CONST_W:CONST_W + T]).then_inc(par_in.sem, 16)
            sp.wait_ge(*wsm_z(0))
            for r, o, w in ((R_F, O_FF, FOX_HEADS), (R_B, O_GB, GDN_HEADS), (R_A, O_GA, GDN_HEADS)):
                sp.dma_start(wsm[:, :, r:r + w], w_in0[:, o:o + w].rearrange("(k p) c -> p k c", p=P))\
                    .then_inc(wsm_in.sem, 16)
            tile_of = lambda w, r0, c0: w[bass.ds(r0, D), bass.ds(c0, P)].rearrange("(k p) c -> p k c", p=P)
            starts = (O_GQ, O_GK, O_GV, O_FQ, O_FK, O_FV, O_GG)
            for j, o in enumerate(starts):
                load(sp, PH_L0, 0, j, tile_of(w_in0, 0, o), None)
            sp.wait_ge(*h_sq(0))
            sp.wait_ge(*h_lo_s(0))
            sp.dma_start(spill, xT[:, :, :].rearrange("p k t -> p (k t)")).then_inc(spilled.sem, 16)
            sp.wait_ge(*row_v(0, 7))
            sp.wait_ge(*row_a(0, 5))
            sp.dma_start(rows_dram, row[0][:, :]).then_inc(row_out.sem, 16)
            with sp.Fori(1, GDN_HEADS) as p:
                for j in (0, 1, 2, 4, 3, 5, 6):
                    load(sp, PH_L0, p, j, tile_of(w_in0, 0, p * P + starts[j]), 7 if j != 3 else None)
            for layer, (ph_o, ph_m, w_out, w1, w2) in enumerate(((PH_OUT0, PH_MLP0, w_out0, w_ff1_0, w_ff2_0),
                                                                 (PH_OUT1, PH_MLP1, w_out1, w_ff1_1, w_ff2_1))):
                if layer:
                    col = lambda g, h: tile_of(w_in1, 0, h * P + g * D)
                    with sp.Fori(0, HG_HEADS) as p:
                        for j, g in enumerate((0, 1, 2, 3)):
                            load(sp, PH_L1, p, j, col(g, p), 4)
                for j in range(KB):
                    back = (7 if j < 7 else None) if layer == 0 else (4 if j < 4 else 36)
                    load(sp, ph_o, 0, j, tile_of(w_out, 0, j * P), back)
                if layer == 0:
                    for s in (so_mm, s_up, fs_s):
                        sp.wait_ge(*s(GDN_HEADS - 1))
                    sp.dma_start(xT[:, :, :].rearrange("p k t -> p (k t)"), spill).then_inc(reloaded.sem, 16)
                with sp.Fori(0, QUARTERS) as q:
                    for j in range(KB):
                        load(sp, ph_m, q, j, tile_of(w1, 0, q * D + j * P), 8)
                    for j in range(KB):
                        load(sp, ph_m, q, KB + j, tile_of(w2, q * D, j * P), 8)
            for d in range(KB):
                sp.wait_ge(*y_ev(0, d + 1))
                sp.dma_start(out[0].rearrange("(t p) d -> p t d", p=P)[:, :, d * P:(d + 1) * P],
                             yn[:, d % 2]).then_inc(stored[d % 2].sem, 16)
            for s in stored:
                sp.wait_ge(s.sem, 16 * KB // 2)
            sp.wait_ge(spilled.sem, 16)
            sp.wait_ge(row_out.sem, 16)

        @block.tensor
        def _(pe):
            ident = cc("ident")
            pe.wait_ge(const_in.sem, 16)
            pe.wait_ge(x_in.sem, 16)
            pe.wait_ge(*b_const(0))
            for k in range(KB):
                if k >= 2:
                    pe.wait_ge(*x_ev(0, k - 1))
                for t in range(TT):
                    last = pe.transpose(mb[k % 2][:, t * P:(t + 1) * P], xn[:, t, k * P:(k + 1) * P], ident)
                last.then_inc(xtr.sem, 1)

            def stat(use):
                pe.wait_ge(*ssq_s(use))
                if use == 0:
                    pe.wait_ge(*x_ev(0))
                pe.matmul(g0[:, :], cc("ones"), ssq[:, :], start=True, stop=True).then_inc(stat_mm.sem, 1)

            stat(0)
            pe.wait_ge(*h_lo_s(0))
            pe.wait_ge(*wsm_lo_s(0))
            for k in range(KB):
                pe.matmul(g1[0:ROWS, :], wsm_hi[:, k], h_hi[:, k], start=(k == 0), stop=False)
                pe.matmul(g1[0:ROWS, :], wsm_lo[:, k], h_hi[:, k], start=False, stop=False)
                last = pe.matmul(g1[0:ROWS, :], wsm_hi[:, k], h_lo[:, k], start=False, stop=(k == KB - 1))
            last.then_inc(row_mm.sem, 1)

            def project0(p, mix=None):
                for s in range(L0_SLICES):
                    products(pe, PH_L0, p, s // KB, s % KB, h_hi, h_lo, None)
                    if mix is not None:
                        run_steps(MIX0[s], pe0, mix)

            def gdn_norm(i):
                for n, b in ((0, g0), (1, g1)):
                    pe.wait_ge(*gsq(i, n + 1))
                    pe.matmul(b[:, :], cc("ones"), (xm, ym)[n][:, :] if n == 0 else ym[:, :, :], start=True, stop=True)\
                        .then_inc(gn_mm.sem, 1)

            def fox_norm(i):
                for n, b in ((0, f0), (1, f1)):
                    pe.wait_ge(*fsq(i, n + 1))
                    pe.matmul(b[:, :], cc("pair_ones"), prob[n][:, :], start=True, stop=True).then_inc(fn_mm.sem, 1)
                pe.wait_ge(*z0_s[5](i))
                if not (isinstance(i, int) and i == 0):
                    pe.wait_ge(*fo_lo(i - 1))
                for t in range(TT):
                    last = pe.transpose(f2[:, t * P:(t + 1) * P], z0[5][:, t * P:(t + 1) * P], ident)
                last.then_inc(fv_tr.sem, 1)

            def gdn_v(i):
                pe.wait_ge(*silu_s(i, 4))
                if not (isinstance(i, int) and i == 0):
                    pe.wait_ge(*go_n(i - 1))
                for t in range(TT):
                    last = pe.transpose(g2[:, t * P:(t + 1) * P], cqkv[2][:, t * P:(t + 1) * P], ident)
                last.then_inc(v_tr.sem, 1)

            def gdn_gram(i):
                pe.wait_ge(*gn_r(i))
                pe.wait_ge(*gn(i))
                for t in range(TT):
                    last = pe.transpose(g0[:, t * P:(t + 1) * P], cqkv[1][:, t * P:(t + 1) * P], ident)
                last.then_inc(k_tr.sem, 1)
                pe.wait_ge(*kbeta_s(i))
                for t in range(TT):
                    c = slice(t * P, (t + 1) * P)
                    last = pe.matmul(g1[:, c], cqkv[1][:, c], kbeta[:, c], start=True, stop=True)
                last.then_inc(gram.sem, 1)
                pe.wait_ge(*vb_s(i))
                for t in range(TT):
                    c = slice(t * P, (t + 1) * P)
                    last = pe.matmul(g2[:, c], cqkv[1][:, c], cqkv[0][:, c], start=True, stop=True)
                last.then_inc(gram.sem, 1)

            def inv0(i):
                pe.wait_ge(*n_s(i))
                pe.wait_ge(*k_nat(i))
                for t in range(TT):
                    last = pe.matmul(g0[:, t * P:(t + 1) * P], nmat[:, t], ident, start=True, stop=True)
                last.then_inc(inv_a.sem, 1)

            def inv_pa(i, l):
                if l == 1:
                    pe.wait_ge(*x_0(i))
                else:
                    pe.wait_ge(*x_up(i, l - 1))
                for t in range(TT):
                    last = pe.matmul(g0[:, t * P:(t + 1) * P], nmat[:, t], xmv[:, t], start=True, stop=True)
                last.then_inc(inv_a.sem, 1)

            def inv_pb(i, l):
                pe.wait_ge(*inv_p(i, l))
                if l == 1:
                    pe.wait_ge(*y_0(i))
                    pe.wait_ge(*qkT_s(i))
                else:
                    pe.wait_ge(*y_up(i, l - 1))
                if l < LEVELS - 1:
                    for t in range(TT):
                        last = pe.matmul(g1[:, t * P:(t + 1) * P], ym[:, t], pm[:, t], start=True, stop=True)
                    last.then_inc(inv_x.sem, 1)
                for t in range(TT):
                    last = pe.matmul(g2[:, t * P:(t + 1) * P], pm[:, t], ym[:, t], start=True, stop=True)
                last.then_inc(inv_y.sem, 1)

            def uw(i):
                pe.wait_ge(*y_up(i))
                for t in range(TT):
                    last = pe.matmul(g0[:, t * P:(t + 1) * P], ym[:, t], vb[:, t], start=True, stop=True)
                last.then_inc(u_mm.sem, 1)
                for t in range(TT):
                    last = pe.matmul(g1[:, t * P:(t + 1) * P], kbg[:, t], ym[:, t], start=True, stop=True)
                last.then_inc(w_mm.sem, 1)

            def scan_v(i, n):
                r = n % 2 * CHUNK
                pe.wait_ge(*s_up(i, n))
                if n == 1:
                    pe.wait_ge(*u_ev(i))
                pe.matmul(g0[r:r + CHUNK, 0:P], pm[:, n // 2, r:r + CHUNK], state[:, :], start=True, stop=True)\
                    .then_inc(sv_mm.sem, 1)

            def scan_s(i, n):
                r, t = n % 2 * CHUNK, n // 2
                c = slice(n * CHUNK, (n + 1) * CHUNK)
                if n:
                    pe.matmul(g2[:, c], state[:, :], qd[:, c], start=True, stop=False)
                pe.wait_ge(*vnew(i, n + 1))
                pe.matmul(g2[:, c], vnv[r:r + CHUNK, t], qkT[r:r + CHUNK, t, r:r + CHUNK], start=(n == 0), stop=True)\
                    .then_inc(so_mm.sem, 1)
                if n < NCH - 1:
                    if n == 0:
                        pe.wait_ge(*w_ev(i))
                    pe.matmul(g1[:, 0:P], kdec[r:r + CHUNK, t], vnv[r:r + CHUNK, t], start=True, stop=True)\
                        .then_inc(ss_mm.sem, 1)

            vnv = t4(cqkv[2])

            def gdn_rms(i):
                pe.wait_ge(*go_sq(i))
                pe.matmul(g0[:, :], cc("ones"), xm[:, :], start=True, stop=True).then_inc(go_mm.sem, 1)

            def fox_s(i, u):
                hh, j = u // TT, u % TT
                h = slice(hh * FOX_DH, (hh + 1) * FOX_DH)
                if u == 0:
                    pe.wait_ge(*fn(i))
                else:
                    pe.wait_ge(*fs_s(i, u))
                n = (j + 1) * P
                pe.matmul(f0[:, 0:n], fqn[h, j * P:n], fkn[h, 0:n], start=True, stop=False)
                pe.matmul(f0[:, j * P:n], ident_b[:, :], neg_b[:, :], start=False, stop=True).then_inc(fs_mm.sem, 1)

            def fox_t(i, u):
                j = u % TT
                pe.wait_ge(*fs_p(i, u + 1))
                if u:
                    pe.wait_ge(*ft_c(i, u))
                for t in range(j + 1):
                    c = slice(t * P, (t + 1) * P)
                    last = pe.transpose(f1[:, c], prob[u % 2][:, c], ident)
                last.then_inc(ft_mm.sem, 1)

            def fox_o(i, u):
                hh, j = u // TT, u % TT
                h = slice(hh * FOX_DH, (hh + 1) * FOX_DH)
                pe.wait_ge(*ft_c(i, u + 1))
                for t in range(j + 1):
                    last = pe.matmul(f2[h, j * P:(j + 1) * P], fvn[:, t, h], probT[:, t], start=(t == 0), stop=(t == j))
                last.then_inc(fo_mm.sem, 1)

            pe0 = {"gdn_norm": gdn_norm, "fox_norm": fox_norm, "gdn_v": gdn_v, "gdn_gram": gdn_gram, "inv0": inv0, "inv_a": inv_pa,
                   "inv_b": inv_pb, "uw": uw, "scan_v": scan_v, "scan_s": scan_s, "gdn_rms": gdn_rms,
                   "fox_s": fox_s, "fox_t": fox_t, "fox_o": fox_o}

            project0(0)
            pe.wait_ge(*row_v(0, 7))
            pe.wait_ge(*row_a(0, 5))
            for n, (b, r) in enumerate(((g1, row[0]), (g2, row[1]))):
                for t in range(TT):
                    last = pe.transpose(b[:, t * ROWS:(t + 1) * ROWS], r[:, t * P:(t + 1) * P], ident[0:ROWS, 0:ROWS])
                last.then_inc(row_tr.sem, 1)
            project0(1, 0)
            with pe.Fori(1, GDN_HEADS - 1) as i:
                project0(i + 1, i)
            for s in range(L0_SLICES):
                run_steps(MIX0[s], pe0, GDN_HEADS - 1)
            gdn_rms(GDN_HEADS - 1)

            def dense_layer(layer, ph_o, ph_m):
                mix_lo = ((go_lo, fo_lo), (hn_lo, hn_lo))[layer]
                for s in mix_lo:
                    pe.wait_ge(*s((GDN_HEADS, HG_HEADS)[layer] - 1))
                for j in range(KB):
                    for k in range(KB):
                        products(pe, ph_o, 0, j, k, a_hi, a_lo, None)
                stat(1 + 2 * layer)

                def quarter(q):
                    for j in range(KB):
                        for k in range(KB):
                            ready = (lambda k: h_lo_s(1 + 2 * layer, k + 1)) if j == 0 else None
                            products(pe, ph_m, q, j, k, h_hi, h_lo, ready)
                    for j in range(KB):
                        for k in range(KB):
                            ready = (lambda k: alo_s[layer](q, k + 1)) if j == 0 else None
                            products(pe, ph_m, q, KB + j, k, a_hi, a_lo, ready)

                with pe.Fori(0, QUARTERS - 1) as q:
                    quarter(q)
                quarter(QUARTERS - 1)

            dense_layer(0, PH_OUT0, PH_MLP0)
            stat(2)

            def project1(p, mix=None):
                for s in range(L1_SLICES):
                    ready = (lambda k: h_lo_s(2, k + 1)) if isinstance(p, int) and s < KB else None
                    products(pe, PH_L1, p, s // KB, s % KB, h_hi, h_lo, ready)
                    if mix is not None:
                        run_steps(MIX1[s], pe1, mix)

            def hg_v(i):
                if not (isinstance(i, int) and i == 0):
                    pe.wait_ge(*hn_ln(i - 1))
                pe.wait_ge(*z1_s[2](i))
                for t in range(TT):
                    last = pe.transpose(g0[:, t * P:(t + 1) * P], z1[2][:, t * P:(t + 1) * P], ident)
                last.then_inc(hv_tr.sem, 1)

            def hg_diag(i):
                pe.wait_ge(*hq_s(i))
                pe.wait_ge(*hk_s(i))
                for t in range(TT):
                    c = slice(t * P, (t + 1) * P)
                    last = pe.matmul(g1[:, c], hk[:, c], hq[:, c], start=True, stop=True)
                last.then_inc(hdg_mm.sem, 1)

            def hg_level(i, l):
                b = (f0, f1)[l % 2]
                pe.wait_ge(*hl_x(i, 2 * l + 2))
                if l >= 2:
                    pe.wait_ge(*hl_c(i, l - 1))
                for t in range(TT):
                    c = slice(t * P, (t + 1) * P)
                    last = pe.matmul(b[:, c], hx[l % 2][:, c], hx[l % 2][:, c], start=True, stop=True)
                last.then_inc(hl_mm.sem, 1)

            def hg_kn(i):
                pe.wait_ge(*hkd_s(i))
                pe.wait_ge(*hv_s(i))
                for t in range(TT):
                    last = pe.transpose(g0[:, t * P:(t + 1) * P], hkd[:, t * P:(t + 1) * P], ident)
                last.then_inc(hkn_tr.sem, 1)

            def hg_kv(i):
                pe.wait_ge(*hkn_s(i))
                pe.wait_ge(*hdg_s(i))
                for h, b in enumerate((g1, g2)):
                    r = h * CHUNK
                    for c in range(TT):
                        last = pe.matmul(b[:, c * P:(c + 1) * P], hkn[r:r + CHUNK, c], hv[r:r + CHUNK, c],
                                         start=True, stop=True)
                    last.then_inc(hkv_mm.sem, 1)

            def hg_o(i):
                pe.wait_ge(*hl_c(i))
                pe.wait_ge(*hqd_s(i))
                for t in range(TT):
                    pe.matmul(f2[:, t * P:(t + 1) * P], hv[:, t], hA[:, t], start=True, stop=False,
                              skip_group_check=True)
                    for n in (2 * t, 2 * t + 1):
                        c = slice(n * CHUNK, (n + 1) * CHUNK)
                        if n:
                            pe.wait_ge(*hS_s(i, n))
                            last = pe.matmul(f2[:, c], hS[:, n], hqd[:, c], start=False, stop=True,
                                             skip_group_check=True)
                last.then_inc(ho_mm.sem, 1)

            def hg_norm(i):
                pe.wait_ge(*ho_sq(i))
                pe.matmul(g0[:, :], cc("ones"), ho[:, :], start=True, stop=True).then_inc(hn_mm.sem, 1)

            pe1 = {"hg_v": hg_v, "hg_diag": hg_diag, "hg_level": hg_level, "hg_kn": hg_kn, "hg_kv": hg_kv, "hg_o": hg_o,
                   "hg_norm": hg_norm}

            project1(0)
            project1(1, 0)
            with pe.Fori(1, HG_HEADS - 1) as i:
                project1(i + 1, i)
            for s in range(L1_SLICES):
                run_steps(MIX1[s], pe1, HG_HEADS - 1)
            hg_norm(HG_HEADS - 1)
            dense_layer(1, PH_OUT1, PH_MLP1)
            for d in range(KB):
                pe.wait_ge(*resid[1](QUARTERS - 1, d + 1))
                if d >= 2:
                    pe.wait_ge(*y_ev(0, d - 1))
                for t in range(TT):
                    last = pe.transpose(mb[d % 2][:, t * P:(t + 1) * P], xT[:, d, t * P:(t + 1) * P], ident)
                last.then_inc(y_tr.sem, 1)

        @block.scalar
        def _(act):
            act.preload_act_table_set(EXP_LN)
            act.wait_ge(const_in.sem, 16)
            act.activation(ident_b[:, :], cc("ident"), ACT.Copy).then_inc(b_const.sem, 1)
            act.activation(neg_b[:, :], cc("fox_neg"), ACT.Copy).then_inc(b_const.sem, 1)
            act.wait_ge(par_in.sem, 32)
            act.wait_ge(wsm_in.sem, 48)
            act.activation(wsm_hi[:, :, :], wsm[:, :, :], ACT.Copy).then_inc(wsm_hi_s.sem, 1)

            def prepare_tile(use, d, ready):
                act.wait_ge(*ready)
                act.activation(h_hi[:, d], xT[:, d], ACT.Copy, scale=pp(gain(use), d)).then_inc(h_hi_s.sem, 1)
                if d >= 2:
                    act.wait_ge(*ssq_s(use, d - 1))
                act.activation(sq[d % 2][:, :], xT[:, d], ACT.Square).then_inc(h_sq.sem, 1)

            def norm(use):
                act.wait_ge(*stat_mm(use))
                act.activation(rstd[:, :], g0[:, :], ACT.Ln, scale=1.0 / D, bias=pp("eps")).then_inc(stat_ln.sem, 1)
                act.wait_ge(*stat_ln(use))
                act.activation(rstd[:, :], rstd[:, :], ACT.Exp, scale=-0.5).then_inc(rstd_s.sem, 1)

            for d in range(KB):
                prepare_tile(0, d, x_ev(0, d + 1))
            norm(0)
            for j in range(LEAD):
                split_hi(act, PH_L0, 0, j)
            r0, r1, r2, r3 = [r[:, :] for r in row]
            act.wait_ge(*row_v(0, 2))
            act.activation(r1, r0, ACT.Abs).then_inc(row_a.sem, 1)
            act.wait_ge(*row_a(0, 1))
            act.activation(r1, r1, ACT.Exp, scale=-1.0).then_inc(row_a.sem, 1)
            act.wait_ge(*row_a(0, 2))
            act.activation(r1, r1, ACT.Ln, bias=cc("ones")[0:ROWS, 0:1]).then_inc(row_a.sem, 1)
            act.activation(small[0:ROWS, 0:1], pp("row_a")[0:ROWS], ACT.Exp).then_inc(row_a.sem, 1)
            act.wait_ge(*row_v(0, 6))
            act.activation(r0[R_B:R_B + GDN_HEADS, :], r2[R_B:R_B + GDN_HEADS, :], ACT.Exp, scale=-1.0)\
                .then_inc(row_a.sem, 1)

            def project0(p, mix=None):
                for j in range(7):
                    early = PH_L0.split_back(j + LEAD) > LEAD
                    for s in range(j * KB, (j + 1) * KB):
                        if early and s % KB == 3:
                            split_hi(act, PH_L0, p, j + LEAD)
                        if mix is not None:
                            run_steps(MIX0[s], act0, mix)
                    if not early:
                        split_hi(act, PH_L0, p, j + LEAD)

            def fox_squares(i):
                act.wait_ge(spilled.sem, 16)
                for n in range(2):
                    act.wait_ge(*z0_s[3 + n](i))
                    act.activation(prob[n][:, :], z0[3 + n][:, :], ACT.Square).then_inc(fsq.sem, 1)

            def silu(i):
                act.wait_ge(*z0_s[6](i))
                if not (isinstance(i, int) and i == 0):
                    act.wait_ge(*go_g(i - 1))
                act.activation(gate[:, :], z0[6][:, :], ACT.Silu).then_inc(silu_s.sem, 1)
                for n in range(3):
                    act.wait_ge(*conv_s(i, CONVOLVED[n]))
                    act.activation(cqkv[n][:, :], cqkv[n][:, :], ACT.Silu).then_inc(silu_s.sem, 1)
                act.preload_act_table_set(EXP_LN)
                for n, b in ((0, xm[:, :]), (1, ym[:, :, :].rearrange("p t c -> p (t c)"))):
                    act.wait_ge(*silu_s(i, 2 + n))
                    act.activation(b, cqkv[n][:, :], ACT.Square).then_inc(gsq.sem, 1)

            def rsqrt(i, bank_, buf, mm, k, ln, r, scale):
                act.wait_ge(*mm(i, k))
                act.activation(buf, bank_[:, :], ACT.Ln, scale=scale, bias=pp("eps")).then_inc(ln.sem, 1)
                act.wait_ge(*ln(i, k))
                act.activation(buf, buf, ACT.Exp, scale=-0.5).then_inc(r.sem, 1)

            def fox_norm(i):
                for n, b in ((0, f0), (1, f1)):
                    rsqrt(i, b, prob[n][:, :], fn_mm, n + 1, fn_ln, fn_r, 1.0 / FOX_DH)
                act.wait_ge(*fv_tr(i))
                act.activation(fvn[:, :, :], t4(f2), ACT.Copy).then_inc(fv_ev.sem, 1)

            def gdn_norm(i):
                for n, b in ((0, g0), (1, g1)):
                    buf = (xm[:, :], ym[:, :, :].rearrange("p t c -> p (t c)"))[n]
                    rsqrt(i, b, buf, gn_mm, n + 1, gn_ln, gn_r, 1.0)

            def decays(i):
                act.wait_ge(*darg_s(i))
                act.activation(dmat[:, :, :], dmat[:, :, :], ACT.Exp).then_inc(dexp_s.sem, 1)
                act.activation(g_bc[:, :], g_bc[:, :], ACT.Exp).then_inc(eg_s.sem, 1)

            def uw(i):
                act.wait_ge(*u_mm(i))
                act.wait_ge(*x_up(i))
                act.activation(xmv, t4(g0), ACT.Copy).then_inc(u_ev.sem, 1)

            def gdn_square(i):
                act.wait_ge(*so_mm(i))
                act.wait_ge(*vnew(i))
                act.activation(xm[:, :], g2[:, :], ACT.Square).then_inc(go_sq.sem, 1)

            def gdn_rms(i):
                rsqrt(i, g0, ym[:, :, :].rearrange("p t c -> p (t c)"), go_mm, 1, go_ln, go_r, 1.0 / DH)

            def gdn_split(i):
                act.wait_ge(*go_g(i))
                act.activation(a_hi[:, bass.ds(i + FOX_W // P, 1)].rearrange("p o t -> p (o t)"),
                               dstr[:, :, :].rearrange("p t c -> p (t c)"), ACT.Copy).then_inc(go_hi.sem, 1)

            def fox_s(i, u):
                n = (u % TT + 1) * P
                act.wait_ge(*fs_nm(i, u + 1))
                act.activation(prob[u % 2][:, 0:n], prob[u % 2][:, 0:n], ACT.Exp, bias=small[:, 4 + u % 2:5 + u % 2],
                               accum_out=small[:, 6 + u % 2:7 + u % 2]).then_inc(fs_e.sem, 1)

            def fox_t(i, u):
                n = (u % TT + 1) * P
                act.wait_ge(*ft_mm(i, u + 1))
                if u:
                    act.wait_ge(*fo_mm(i, u))
                act.activation(probT[:, 0:u % TT + 1], f1[:, 0:n].rearrange("p (t c) -> p t c", c=P), ACT.Copy)\
                    .then_inc(ft_c.sem, 1)

            def fox_out(i):
                act.wait_ge(*fo_mm(i))
                act.activation(a_hi[:, bass.ds(i, 1)].rearrange("p o t -> p (o t)"), f2[:, :], ACT.Copy)\
                    .then_inc(fo_hi.sem, 1)

            act0 = {"fox_squares": fox_squares, "silu": silu, "fox_norm": fox_norm, "gdn_norm": gdn_norm,
                    "decays": decays, "uw": uw, "gdn_out": gdn_square, "gdn_rms": gdn_rms, "gdn_split": gdn_split,
                    "fox_s": fox_s, "fox_t": fox_t, "fox_out": fox_out}

            project0(0)
            act.wait_ge(*row_tr(0, 1))
            act.activation(nat[:, :, :], g1[:, 0:TT * ROWS].rearrange("p (t r) -> p t r", r=ROWS), ACT.Copy)\
                .then_inc(row_a.sem, 1)
            act.wait_ge(*row_tr(0, 2))
            gd = g2[:, 0:TT * ROWS].rearrange("p (t r) -> p t r", r=ROWS)
            act.activation(kd_scale[:, :, :], gd[:, :, R_A:R_A + GDN_HEADS], ACT.Exp).then_inc(row_a.sem, 1)
            act.wait_ge(*row_a(0, 6))
            act.activation(kb_scale[:, :, :], nat[:, :, R_A:R_A + GDN_HEADS], ACT.Exp).then_inc(row_a.sem, 1)
            project0(1, 0)
            with act.Fori(1, GDN_HEADS - 1) as i:
                project0(i + 1, i)
            for s in range(L0_SLICES):
                run_steps(MIX0[s], act0, GDN_HEADS - 1)
            gdn_rms(GDN_HEADS - 1)
            gdn_split(GDN_HEADS - 1)

            def dense_layer(layer, ph_o, ph_m):
                for j in range(KB):
                    split_hi(act, ph_o if j + LEAD < KB else ph_m, 0, (j + LEAD) % KB)
                    prepare_tile(1 + 2 * layer, j, x_out[layer](0, j + 1))
                norm(1 + 2 * layer)

                def quarter(q, last=False):
                    for j in range(2 * KB):
                        if not (last and layer == 1 and j + LEAD >= 2 * KB):
                            split_hi(act, ph_m, q, j + LEAD)
                        if j < KB:
                            act.wait_ge(*relu_s[layer](q, j + 1))
                            if j >= 2:
                                act.wait_ge(*alo_s[layer](q, j - 1))
                            act.activation(act2[j % 2][:, :], relu[j % 2][:, :], ACT.Square).then_inc(sq_s[layer].sem, 1)
                            act.activation(a_hi[:, j], relu[j % 2][:, :], ACT.Square).then_inc(ahi_s[layer].sem, 1)
                        elif last and layer == 0:
                            prepare_tile(2, j - KB, resid[0](QUARTERS - 1, j - KB + 1))

                with act.Fori(0, QUARTERS - 1) as q:
                    quarter(q)
                quarter(QUARTERS - 1, True)

            dense_layer(0, PH_OUT0, PH_MLP0)
            norm(2)
            act.wait_ge(*lb_v(0, 3))
            act.activation(lbs[:, 0], lbs[:, 0], ACT.Exp).then_inc(lb_a.sem, 1)
            act.activation(lbs[:, 1], lbs[:, 1], ACT.Exp).then_inc(lb_a.sem, 1)

            def project1(p, mix=None):
                for j in range(4):
                    for s in range(j * KB, (j + 1) * KB):
                        if s % KB == (5 if mix is not None else 0):
                            split_hi(act, PH_L1, p, j + LEAD)
                        if mix is not None:
                            run_steps(MIX1[s], act1, mix)

            def hg_f(i):
                act.wait_ge(*z1_s[1](i))
                act.activation(hf[:, :], z1[1][:, :], ACT.Exp, scale=-1.0).then_inc(hexp_s.sem, 1)

            def hg_silu(i):
                act.wait_ge(*z1_s[0](i))
                act.activation(hq[:, :], z1[0][:, :], ACT.Silu).then_inc(hq_s.sem, 1)
                act.wait_ge(*z1_s[3](i))
                if not (isinstance(i, int) and i == 0):
                    act.wait_ge(*hgk_s(i - 1))
                act.activation(hg[:, :], z1[3][:, :], ACT.Silu).then_inc(hg_s.sem, 1)
                act.preload_act_table_set(EXP_LN)

            def hg_log(i):
                act.wait_ge(*hf_s(i))
                act.activation(hb[:, :], hf[:, :], ACT.Ln).then_inc(hln_s.sem, 1)
                act.wait_ge(*hb_s(i))
                act.activation(hdec[:, :], hf[:, :], ACT.Exp).then_inc(heb_s.sem, 1)
                act.wait_ge(*hka_s(i))
                act.activation(hkd[:, :], hkd[:, :], ACT.Exp).then_inc(hke_s.sem, 1)

            def hg_v(i):
                act.wait_ge(*hv_tr(i))
                act.activation(hv[:, :, :], t4(g0), ACT.Copy).then_inc(hv_s.sem, 1)

            def hg_exp(i, l):
                act.wait_ge(*hl_d(i, 2 * l + 2))
                act.activation(he[l % 2][:, :], he[l % 2][:, :], ACT.Exp).then_inc(hl_e.sem, 1)

            def hg_kn(i):
                act.wait_ge(*hkn_tr(i))
                act.activation(hkn[:, :, :], t4(g0), ACT.Copy).then_inc(hkn_s.sem, 1)

            def hg_square(i):
                act.wait_ge(*ho_mm(i))
                act.wait_ge(*hl_x(i))
                act.activation(ho[:, :], f2[:, :], ACT.Square).then_inc(ho_sq.sem, 1)

            def hg_norm(i):
                act.wait_ge(*hn_mm(i))
                act.activation(ho[:, :], g0[:, :], ACT.Ln, scale=1.0 / DH, bias=pp("eps")).then_inc(hn_ln.sem, 1)
                act.wait_ge(*hn_ln(i))
                act.activation(ho[:, :], ho[:, :], ACT.Exp, scale=-0.5).then_inc(hn_r.sem, 1)

            def hg_norm_split(i):
                act.wait_ge(*hn_g(i))
                act.activation(a_hi[:, bass.ds(i, 1)].rearrange("p o t -> p (o t)"), hgo[:, :], ACT.Copy)\
                    .then_inc(hn_hi.sem, 1)

            act1 = {"hg_f": hg_f, "hg_silu": hg_silu, "hg_log": hg_log, "hg_v": hg_v, "hg_exp": hg_exp,
                    "hg_kn": hg_kn, "hg_square": hg_square, "hg_norm": hg_norm, "hg_norm_split": hg_norm_split}

            project1(0)
            project1(1, 0)
            with act.Fori(1, HG_HEADS - 1) as i:
                project1(i + 1, i)
            for s in range(L1_SLICES):
                run_steps(MIX1[s], act1, HG_HEADS - 1)
            hg_norm(HG_HEADS - 1)
            hg_norm_split(HG_HEADS - 1)
            dense_layer(1, PH_OUT1, PH_MLP1)

        @block.vector
        def _(dve):
            for k in range(KB):
                dve.wait_ge(*xtr(0, k + 1))
                dve.tensor_copy(xT[:, k], mb[k % 2][:, :]).then_inc(x_ev.sem, 1)

            for n in range(3):
                dve.memset(z0[n][:, 0:3], 0.0).then_inc(pads.sem, 1)

            def rest(use, d):
                dve.wait_ge(*h_hi_s(use, d + 1))
                dve.scalar_tensor_tensor(h_lo[:, d], xT[:, d], pp(gain(use), d), h_hi[:, d].bitcast(F32),
                                         ALU.mult, ALU.subtract).then_inc(h_lo_s.sem, 1)

            for d in range(KB):
                rest(0, d)
            dve.wait_ge(*wsm_hi_s(0))
            dve.tensor_tensor(wsm_lo[:, :, :], wsm[:, :, :], wsm_hi[:, :, :].bitcast(F32), ALU.subtract)\
                .then_inc(wsm_lo_s.sem, 1)
            for j in range(LEAD):
                split_lo(dve, PH_L0, 0, j)
            r0, r1, r2, r3 = [r[:, :] for r in row]
            rp = slice(0, ROWS)
            dve.wait_ge(*row_mm(0))
            dve.wait_ge(*rstd_s(0))
            dve.tensor_tensor(r0, g1[rp, :], rstd[rp, :], ALU.mult).then_inc(row_v.sem, 1)
            dve.wait_ge(*row_v(0, 1))
            dve.tensor_scalar(r0, r0, pp("row_bias")[rp], pp("row_sign")[rp], ALU.add, ALU.mult).then_inc(row_v.sem, 1)
            dve.wait_ge(*row_a(0, 3))
            dve.scalar_tensor_tensor(r2, r0, 0.0, r1, ALU.max, ALU.add).then_inc(row_v.sem, 1)
            dve.wait_ge(*row_a(0, 4))
            dve.tensor_scalar(small[rp, 1:2], small[rp, 0:1], -1.0, None, ALU.mult).then_inc(row_v.sem, 1)
            dve.wait_ge(*row_v(0, 4))
            dve.tensor_scalar(r3, r2, small[rp, 1:2], None, ALU.mult).then_inc(row_v.sem, 1)
            dve.wait_ge(*row_v(0, 5))
            dve.tensor_tensor_scan(r0, row_reset[rp, :], r3, 0.0, ALU.mult, ALU.add).then_inc(row_v.sem, 1)
            dve.wait_ge(*row_v(0, 6))
            r0c = r0.rearrange("p (c t) -> p c t", t=CHUNK)
            dve.wait_ge(*row_a(0, 5))
            dve.tensor_tensor(r1.rearrange("p (c t) -> p c t", t=CHUNK),
                              r0c[:, :, CHUNK - 1:CHUNK].to_broadcast([ROWS, NCH, CHUNK]), r0c, ALU.subtract)\
                .then_inc(row_v.sem, 1)

            def evac0(p, j):
                b = dense[j % 2]
                dve.wait_ge(gemm_done.sem, PH_L0.n(p, j) + 1)
                if not (isinstance(p, int) and p == 0):
                    if j < 3:
                        dve.wait_ge(*conv_s(p - 1, CONVOLVED[j]))
                    elif j < 5:
                        dve.wait_ge(*fn(p - 1, j - 2))
                    elif j == 5:
                        dve.wait_ge(*fv_tr(p - 1))
                    else:
                        dve.wait_ge(*silu_s(p - 1, 1))
                dst = z0[j][:, 3:3 + T] if j < 3 else z0[j][:, :]
                dve.tensor_tensor(dst, b[:, :], rstd[:, :], ALU.mult).then_inc(z0_s[j].sem, 1)

            def project0(p, mix=None):
                for j in range(7):
                    if mix is not None:
                        for s in range(j * KB, (j + 1) * KB):
                            run_steps(MIX0[s], dve0, mix)
                    evac0(p, j)
                    dve.wait_ge(*z0_s[j](p))
                    dve.sem_inc(evac_done.sem, 1)
                    split_lo(dve, PH_L0, p, j + LEAD)

            def conv_taps(i, which, before):
                a, _ = _p["conv"]
                for tap in range(3, -1, -1):
                    for n in which:
                        w = par[:, bass.ds(i + (a + (tap * 3 + n) * GDN_HEADS), 1)]
                        if tap == 3:
                            dve.wait_ge(*z0_s[n](i))
                            dve.tensor_scalar(cqkv[n][:, :], z0[n][:, 3:3 + T], w, None, ALU.mult)\
                                .then_inc(conv_s.sem, 1)
                        else:
                            dve.wait_ge(*conv_s(i, before + len(which) * (2 - tap) + which.index(n) + 1))
                            dve.scalar_tensor_tensor(cqkv[n][:, :], z0[n][:, tap:tap + T], w, cqkv[n][:, :],
                                                     ALU.mult, ALU.add).then_inc(conv_s.sem, 1)

            def conv_qk(i):
                dve.wait_ge(spilled.sem, 16)
                conv_taps(i, (0, 1), 0)

            def conv_v(i):
                conv_taps(i, (2,), 8)

            def fox_norm(i):
                for n, (z, o, g) in enumerate(((z0[3], fqn, small[:, 2:3]), (z0[4], fkn, pp("fkn")))):
                    dve.wait_ge(*fn_r(i, n + 1))
                    dve.scalar_tensor_tensor(o[:, :], z[:, :], g, prob[n][:, :], ALU.mult, ALU.mult)\
                        .then_inc(fn.sem, 1)

            def gdn_norm(i):
                dve.wait_ge(*gn_r(i, 1))
                dve.scalar_tensor_tensor(cqkv[0][:, :], cqkv[0][:, :], float(DH) ** -0.5, xm[:, :], ALU.mult, ALU.mult)\
                    .then_inc(gn.sem, 1)
                dve.wait_ge(*gn_r(i, 2))
                dve.tensor_tensor(cqkv[1][:, :], cqkv[1][:, :], ym[:, :, :].rearrange("p t c -> p (t c)"), ALU.mult)\
                    .then_inc(gn.sem, 1)

            def decays(i):
                dve.wait_ge(g_in.sem, i * 16 + 16)
                for t in range(TT):
                    dve.scalar_tensor_tensor(dmat[:, t], g_bc[:, t * P:(t + 1) * P],
                                             nat[:, t, bass.ds(i + R_A, 1)], cc("causal_neg"),
                                             ALU.subtract, ALU.add).then_inc(darg_s.sem, 1)

            def gdn_scaled(i):
                dve.wait_ge(b_in.sem, i * 16 + 16)
                dve.wait_ge(*gn(i))
                dve.tensor_tensor(kbeta[:, :], cqkv[1][:, :], b_bc[:, :], ALU.mult).then_inc(kbeta_s.sem, 1)
                dve.wait_ge(*eg_s(i))
                dve.tensor_tensor(qd[:, :], cqkv[0][:, :], g_bc[:, :], ALU.mult).then_inc(qd_s.sem, 1)

            def per_frame(a, i, at_=0):
                return a[:, :, bass.ds(i + at_, 1)].to_broadcast([P, TT, P])

            def gdn_v(i):
                dve.wait_ge(*v_tr(i))
                dve.tensor_tensor(vb[:, :, :], t4(g2), per_frame(nat, i, R_B), ALU.mult).then_inc(vb_s.sem, 1)

            def gdn_gram(i):
                dve.wait_ge(*k_tr(i))
                dve.tensor_tensor(kbg[:, :, :], t4(g0), per_frame(kb_scale, i), ALU.mult).then_inc(k_nat.sem, 1)
                dve.tensor_tensor(kdec[:, :, :], t4(g0), per_frame(kd_scale, i), ALU.mult).then_inc(k_nat.sem, 1)
                dve.wait_ge(*gram(i, 1))
                dve.wait_ge(*dstr_s(i))
                dve.tensor_tensor(nmat[:, :, :], t4(g1), dstr[:, :, :], ALU.mult).then_inc(n_s.sem, 1)
                dve.wait_ge(*gram(i, 2))
                dve.tensor_tensor(qkT[:, :, :], t4(g2), dmat[:, :, :], ALU.mult).then_inc(qkT_s.sem, 1)

            def tiles(name):
                a, w = _c[name]
                return cst[:, a:a + w].rearrange("p (o c) -> p o c", o=1).to_broadcast([P, TT, P])

            def inv0(i):
                dve.wait_ge(*n_s(i))
                dve.wait_ge(*gram(i, 1))
                dve.tensor_tensor(ym[:, :, :], nmat[:, :, :], tiles("up0"), ALU.mult).then_inc(y_0.sem, 1)
                dve.wait_ge(*y_0(i, 1))
                dve.tensor_tensor(ym[:, :, :], tiles("ident"), ym[:, :, :], ALU.subtract).then_inc(y_0.sem, 1)
                dve.wait_ge(*inv_a(i, 1))
                dve.tensor_tensor(xmv, t4(g0), tiles("low0"), ALU.mult).then_inc(x_0.sem, 1)
                dve.wait_ge(*x_0(i, 1))
                dve.tensor_tensor(xmv, tiles("ident"), xmv, ALU.subtract).then_inc(x_0.sem, 1)

            def inv_da(i, l):
                dve.wait_ge(*inv_a(i, l + 1))
                dve.tensor_tensor(pm[:, :, :], t4(g0), tiles(f"low{l}"), ALU.mult).then_inc(inv_p.sem, 1)

            def inv_db(i, l):
                if l < LEVELS - 1:
                    dve.wait_ge(*inv_x(i, l))
                    dve.tensor_tensor(xmv, xmv, t4(g1), ALU.subtract).then_inc(x_up.sem, 1)
                dve.wait_ge(*inv_y(i, l))
                dve.tensor_tensor(ym[:, :, :], ym[:, :, :], t4(g2), ALU.subtract).then_inc(y_up.sem, 1)

            def uw(i):
                dve.wait_ge(*w_mm(i))
                dve.tensor_copy(pm[:, :, :], t4(g1)).then_inc(w_ev.sem, 1)

            vnv = t4(cqkv[2])

            def scan_v(i, n):
                r, t = n % 2 * CHUNK, n // 2
                dve.wait_ge(*sv_mm(i, n))
                dve.tensor_tensor(vnv[r:r + CHUNK, t], xmv[r:r + CHUNK, t], g0[r:r + CHUNK, 0:P], ALU.subtract)\
                    .then_inc(vnew.sem, 1)

            def scan_s(i, n):
                if n == 0:
                    dve.wait_ge(*u_ev(i))
                    dve.wait_ge(*v_tr(i))
                    dve.tensor_copy(vnv[0:CHUNK, 0], xmv[0:CHUNK, 0]).then_inc(vnew.sem, 1)
                    dve.wait_ge(*ss_mm(i, 1))
                    dve.tensor_copy(state[:, :], g1[:, 0:P]).then_inc(s_up.sem, 1)
                elif n < NCH - 1:
                    dve.wait_ge(*ss_mm(i, n + 1))
                    dve.wait_ge(*s_up(i, n))
                    last = (n + 1) * CHUNK - 1
                    dve.scalar_tensor_tensor(state[:, :], state[:, :], g_bc[:, last:last + 1], g1[:, 0:P],
                                             ALU.mult, ALU.add).then_inc(s_up.sem, 1)

            def gdn_rms(i):
                dve.wait_ge(*go_r(i))
                dve.scalar_tensor_tensor(pm[:, :, :], t4(g2), pp("gdn_o"), ym[:, :, :], ALU.mult, ALU.mult)\
                    .then_inc(go_n.sem, 1)

            def gdn_split(i):
                dve.wait_ge(*go_hi(i))
                dve.tensor_tensor(a_lo[:, bass.ds(i + FOX_W // P, 1)].rearrange("p o t -> p (o t)"),
                                  dstr[:, :, :].rearrange("p t c -> p (t c)"),
                                  a_hi[:, bass.ds(i + FOX_W // P, 1)].rearrange("p o t -> p (o t)").bitcast(F32),
                                  ALU.subtract).then_inc(go_lo.sem, 1)

            def fox_s(i, u):
                hh, j = u // TT, u % TT
                n = (j + 1) * P
                dve.wait_ge(*fs_mm(i, u + 1))
                if u == 0:
                    for c in c_in:
                        dve.wait_ge(c.sem, i * 16 + 16)
                    dve.wait_ge(*fn(i))
                if u >= 2:
                    dve.wait_ge(*ft_mm(i, u - 1))
                dve.scalar_tensor_tensor(prob[u % 2][:, 0:n], f0[:, 0:n], nat[:, j, bass.ds(i * 2 + hh, 1)],
                                         c_bc[hh][:, 0:n], ALU.add, ALU.subtract).then_inc(fs_s.sem, 1)
                dve.wait_ge(*fs_s(i, u + 1))
                dve.reduce_max(small[:, 8 + u % 2:9 + u % 2], prob[u % 2][:, 0:n], AX.X).then_inc(fs_m.sem, 1)
                dve.wait_ge(*fs_m(i, u + 1))
                if u >= 2:
                    dve.wait_ge(*fs_e(i, u - 1))
                dve.tensor_scalar(small[:, 4 + u % 2:5 + u % 2], small[:, 8 + u % 2:9 + u % 2], -1.0, None, ALU.mult)\
                    .then_inc(fs_nm.sem, 1)

            def fox_recip(i, u):
                dve.wait_ge(*fs_e(i, u + 1))
                if u >= 2:
                    dve.wait_ge(*fs_p(i, u - 1))
                dve.reciprocal(small[:, 10 + u % 2:11 + u % 2], small[:, 6 + u % 2:7 + u % 2]).then_inc(fs_r.sem, 1)

            def fox_out(i):
                dve.wait_ge(*fo_hi(i))
                dve.tensor_tensor(a_lo[:, bass.ds(i, 1)].rearrange("p o t -> p (o t)"), f2[:, :],
                                  a_hi[:, bass.ds(i, 1)].rearrange("p o t -> p (o t)").bitcast(F32), ALU.subtract)\
                    .then_inc(fo_lo.sem, 1)

            dve0 = {"conv_qk": conv_qk, "conv_v": conv_v, "gdn_rms": gdn_rms, "gdn_split": gdn_split,
                    "fox_norm": fox_norm, "gdn_norm": gdn_norm, "decays": decays,
                    "gdn_v": gdn_v, "gdn_scaled": gdn_scaled, "gdn_gram": gdn_gram, "inv0": inv0, "inv_a": inv_da, "inv_b": inv_db, "uw": uw,
                    "scan_v": scan_v, "scan_s": scan_s, "fox_s": fox_s, "fox_recip": fox_recip,
                    "fox_out": fox_out}

            dve.wait_ge(par_in.sem, 32)
            dve.wait_ge(*pads(0))
            dve.tensor_scalar(small[:, 2:3], pp("fqn"), float(FOX_DH) ** -0.5, None, ALU.mult).then_inc(row_v.sem, 1)
            dve.wait_ge(*row_v(0, 8))
            project0(0)
            dve.wait_ge(*row_a(0, 8))
            dve.tensor_tensor(kb_scale[:, :, :], kb_scale[:, :, :], nat[:, :, R_B:R_B + GDN_HEADS], ALU.mult)\
                .then_inc(row_v.sem, 1)
            dve.wait_ge(*row_v(0, 9))
            project0(1, 0)
            with dve.Fori(1, GDN_HEADS - 1) as i:
                project0(i + 1, i)
            for s in range(L0_SLICES):
                run_steps(MIX0[s], dve0, GDN_HEADS - 1)
            gdn_rms(GDN_HEADS - 1)
            gdn_split(GDN_HEADS - 1)

            def dense_layer(layer, ph_o, ph_m):
                use = 1 + 2 * layer
                for j in range(KB):
                    if layer == 0 and j == 0:
                        dve.wait_ge(reloaded.sem, 16)
                    dve.wait_ge(gemm_done.sem, ph_o.n(0, j) + 1)
                    dve.tensor_tensor(xT[:, j], xT[:, j], dense[j % 2][:, :], ALU.add).then_inc(x_out[layer].sem, 1)
                    dve.wait_ge(*x_out[layer](0, j + 1))
                    dve.sem_inc(evac_done.sem, 1)
                    split_lo(dve, ph_o if j + LEAD < KB else ph_m, 0, (j + LEAD) % KB)
                    rest(use, j)
                dve.wait_ge(*rstd_s(use))

                def quarter(q, last=False):
                    for j in range(2 * KB):
                        b = dense[j % 2]
                        dve.wait_ge(gemm_done.sem, ph_m.n(q, j) + 1)
                        if j < KB:
                            if j >= 2:
                                dve.wait_ge(*ahi_s[layer](q, j - 1))
                            dve.scalar_tensor_tensor(relu[j % 2][:, :], b[:, :], 0.0, rstd[:, :], ALU.max, ALU.mult)\
                                .then_inc(relu_s[layer].sem, 1)
                            dve.wait_ge(*relu_s[layer](q, j + 1))
                            dve.sem_inc(evac_done.sem, 1)
                            split_lo(dve, ph_m, q, j + LEAD)
                            dve.wait_ge(*ahi_s[layer](q, j + 1))
                            dve.tensor_tensor(a_lo[:, j], act2[j % 2][:, :], a_hi[:, j].bitcast(F32), ALU.subtract)\
                                .then_inc(alo_s[layer].sem, 1)
                        else:
                            d = j - KB
                            dve.tensor_tensor(xT[:, d], xT[:, d], b[:, :], ALU.add).then_inc(resid[layer].sem, 1)
                            dve.wait_ge(*resid[layer](q, d + 1))
                            dve.sem_inc(evac_done.sem, 1)
                            if not (last and layer == 1 and j + LEAD >= 2 * KB):
                                split_lo(dve, ph_m, q, j + LEAD)
                            if last and layer == 0:
                                rest(2, d)

                with dve.Fori(0, QUARTERS - 1) as q:
                    quarter(q)
                quarter(QUARTERS - 1, True)

            dense_layer(0, PH_OUT0, PH_MLP0)
            l0, l1 = pp("lb0", 0, HG_HEADS), pp("lb1", 0, HG_HEADS)
            dve.tensor_tensor(lbs[:, 2], l0, l1, ALU.max).then_inc(lb_v.sem, 1)
            dve.wait_ge(*lb_v(0, 1))
            dve.tensor_tensor(lbs[:, 0], l0, lbs[:, 2], ALU.subtract).then_inc(lb_v.sem, 1)
            dve.tensor_tensor(lbs[:, 1], l1, lbs[:, 2], ALU.subtract).then_inc(lb_v.sem, 1)
            dve.wait_ge(*lb_a(0))
            dve.tensor_tensor(lbs[:, 2], lbs[:, 0], lbs[:, 1], ALU.add).then_inc(lb_v.sem, 1)
            dve.wait_ge(*lb_v(0, 4))
            dve.reciprocal(lbs[:, 3], lbs[:, 2]).then_inc(lb_v.sem, 1)
            dve.wait_ge(*lb_v(0, 5))
            dve.tensor_tensor(lbs[:, 1], lbs[:, 1], lbs[:, 3], ALU.mult).then_inc(lb_v.sem, 1)
            dve.wait_ge(*lb_v(0, 6))
            dve.tensor_scalar(lbs[:, 2], lbs[:, 1], -1.0, 1.0, ALU.mult, ALU.add).then_inc(lb_v.sem, 1)
            dve.wait_ge(*lb_v(0, 7))
            dve.wait_ge(*rstd_s(2))

            def project1(p, mix=None):
                for j in range(4):
                    if mix is not None:
                        for s in range(j * KB, (j + 1) * KB):
                            run_steps(MIX1[s], dve1, mix)
                    dve.wait_ge(gemm_done.sem, PH_L1.n(p, j) + 1)
                    if not (isinstance(p, int) and p == 0):
                        dve.wait_ge(*(hq_s, hexp_s, hv_tr, hg_s)[j](p - 1))
                    dve.tensor_tensor(z1[j][:, :], dense[j % 2][:, :], rstd[:, :], ALU.mult).then_inc(z1_s[j].sem, 1)
                    dve.wait_ge(*z1_s[j](p))
                    dve.sem_inc(evac_done.sem, 1)
                    split_lo(dve, PH_L1, p, j + LEAD)

            def chunks(a, m=CHUNK):
                return a[:, :].rearrange("p (c t) -> p c t", t=m)

            def hg_f(i):
                dve.wait_ge(*hexp_s(i))
                dve.tensor_scalar(hdec[:, :], hf[:, :], 1.0, None, ALU.add).then_inc(hd_s.sem, 1)
                dve.wait_ge(*hd_s(i))
                dve.reciprocal(hkd[:, :], hdec[:, :]).then_inc(hr_s.sem, 1)
                dve.wait_ge(*hr_s(i))
                dve.tensor_scalar(hf[:, :], hkd[:, :], lbs[:, 2, bass.ds(i, 1)], lbs[:, 1, bass.ds(i, 1)],
                                  ALU.mult, ALU.add).then_inc(hf_s.sem, 1)
                dve.wait_ge(*hf_s(i))
                dve.tensor_scalar(hk[:, :], hf[:, :], -1.0, 1.0, ALU.mult, ALU.add).then_inc(hk_s.sem, 1)

            def hg_log(i):
                dve.wait_ge(*hk_s(i))
                dve.wait_ge(*hln_s(i))
                dve.tensor_tensor_scan(hf[:, :], cc("chunk_reset"), hb[:, :], 0.0, ALU.mult, ALU.add)\
                    .then_inc(hb_s.sem, 1)
                dve.wait_ge(*hb_s(i))
                dve.tensor_tensor(chunks(hkd), chunks(hf)[:, :, CHUNK - 1:CHUNK].to_broadcast([P, NCH, CHUNK]),
                                  chunks(hf), ALU.subtract).then_inc(hka_s.sem, 1)
                dve.wait_ge(*heb_s(i))
                dve.tensor_tensor(hqd[:, :], hq[:, :], hdec[:, :], ALU.mult).then_inc(hqd_s.sem, 1)
                dve.wait_ge(*hke_s(i))
                dve.tensor_tensor(hkd[:, :], hkd[:, :], hk[:, :], ALU.mult).then_inc(hkd_s.sem, 1)

            def hg_diag_own(i):
                dve.wait_ge(*hdg_mm(i))
                dve.tensor_tensor(hA[:, :, :], t4(g1), tiles("ident"), ALU.mult).then_inc(hdg_s.sem, 1)

            def hg_scale(i, l):
                h = 1 << l
                e, xx = chunks(he[l % 2], 2 * h), chunks(hx[l % 2], 2 * h)
                dve.wait_ge(*hl_e(i, l + 1))
                if l == 0 and not (isinstance(i, int) and i == 0):
                    dve.wait_ge(*hn_g(i - 1))
                if l >= 2:
                    dve.wait_ge(*hl_mm(i, l - 1))
                dve.tensor_tensor(xx[:, :, 0:h], chunks(hk, 2 * h)[:, :, 0:h], e[:, :, 0:h], ALU.mult).then_inc(hl_x.sem, 1)
                dve.tensor_tensor(xx[:, :, h:], chunks(hq, 2 * h)[:, :, h:], e[:, :, h:], ALU.mult).then_inc(hl_x.sem, 1)

            def hg_merge(i, l):
                dve.wait_ge(const_in.sem, 16)
                dve.wait_ge(*hl_mm(i, l + 1))
                dve.wait_ge(*(hl_c(i, l) if l else hdg_s(i)))
                dve.copy_predicated(hA[:, :, :], tiles(f"up{l}").bitcast(U32), t4((f0, f1)[l % 2]))\
                    .then_inc(hl_c.sem, 1)

            def hg_state(i):
                for n in range(1, NCH):
                    b = (g1, g2)[(n - 1) % 2]
                    c = (n - 1) // 2
                    if n <= 2:
                        dve.wait_ge(*hkv_mm(i, n))
                    if n == 1:
                        dve.tensor_copy(hS[:, 1], b[:, 0:P]).then_inc(hS_s.sem, 1)
                    else:
                        dve.wait_ge(*hS_s(i, n - 1))
                        last = n * CHUNK - 1
                        dve.scalar_tensor_tensor(hS[:, n], hS[:, n - 1], hdec[:, last:last + 1],
                                                 b[:, c * P:(c + 1) * P], ALU.mult, ALU.add).then_inc(hS_s.sem, 1)

            def hg_norm(i):
                dve.wait_ge(*hn_r(i))
                dve.tensor_tensor(hx[0][:, :], f2[:, :], ho[:, :], ALU.mult).then_inc(hn_t.sem, 1)

            def hg_norm_split(i):
                dve.wait_ge(*hn_hi(i))
                dve.tensor_tensor(a_lo[:, bass.ds(i, 1)].rearrange("p o t -> p (o t)"), hgo[:, :],
                                  a_hi[:, bass.ds(i, 1)].rearrange("p o t -> p (o t)").bitcast(F32), ALU.subtract)\
                    .then_inc(hn_lo.sem, 1)

            dve1 = {"hg_f": hg_f, "hg_log": hg_log, "hg_diag_own": hg_diag_own, "hg_scale": hg_scale, "hg_state": hg_state,
                    "hg_merge": hg_merge, "hg_norm": hg_norm, "hg_norm_split": hg_norm_split}

            project1(0)
            project1(1, 0)
            with dve.Fori(1, HG_HEADS - 1) as i:
                project1(i + 1, i)
            for s in range(L1_SLICES):
                run_steps(MIX1[s], dve1, HG_HEADS - 1)
            hg_norm(HG_HEADS - 1)
            hg_norm_split(HG_HEADS - 1)
            dense_layer(1, PH_OUT1, PH_MLP1)
            for d in range(KB):
                dve.wait_ge(*y_tr(0, d + 1))
                if d >= 2:
                    dve.wait_ge(stored[d % 2].sem, 16 * (d // 2))
                dve.tensor_copy(yn[:, d % 2], t4(mb[d % 2])).then_inc(y_ev.sem, 1)

        @block.gpsimd
        def _(pool):
            pool.memset(wsm[:, :, :], 0.0).then_inc(wsm_z.sem, 1)

            def sum_squares(use):
                for d in range(KB):
                    pool.wait_ge(*h_sq(use, d + 1))
                    if d == 0:
                        pool.tensor_copy(ssq[:, :], sq[0][:, :]).then_inc(ssq_s.sem, 1)
                    else:
                        pool.wait_ge(*ssq_s(use, d))
                        pool.tensor_tensor(ssq[:, :], ssq[:, :], sq[d % 2][:, :], ALU.add).then_inc(ssq_s.sem, 1)

            sum_squares(0)

            def spread(dst, row_, arrived):
                pool.dma_start(dst[:, :], rows_dram[bass.ds(row_, 1), :].partition_broadcast(P)
                               .rearrange("p o t -> p (o t)")).then_inc(arrived.sem, 16)

            def fox_rows(i):
                if not (isinstance(i, int) and i == 0):
                    pool.wait_ge(*fs_s(i - 1))
                spread(c_bc[0], i * 2 + R_F, c_in[0])
                spread(c_bc[1], i * 2 + (R_F + 1), c_in[1])

            def gdn_rows(i):
                if not (isinstance(i, int) and i == 0):
                    pool.wait_ge(*s_up(i - 1))
                spread(g_bc, i + R_A, g_in)
                spread(b_bc, i + R_B, b_in)

            def strict_decays(i):
                a, w = _c["strict"]
                pool.wait_ge(*dexp_s(i))
                pool.tensor_tensor(dstr[:, :, :], dmat[:, :, :],
                                   cst[:, a:a + w].rearrange("p (o c) -> p o c", o=1).to_broadcast([P, TT, P]),
                                   ALU.mult).then_inc(dstr_s.sem, 1)

            def fox_probs(i, u):
                n = (u % TT + 1) * P
                pool.wait_ge(*fs_r(i, u + 1))
                pool.tensor_tensor(prob[u % 2][:, 0:n], prob[u % 2][:, 0:n],
                                   small[:, 10 + u % 2:11 + u % 2].to_broadcast([P, n]), ALU.mult)\
                    .then_inc(fs_p.sem, 1)

            def gdn_rms(i):
                pool.wait_ge(*go_n(i))
                pool.wait_ge(*n_s(i))
                pool.tensor_tensor(dstr[:, :, :].rearrange("p t c -> p (t c)"),
                                   pm[:, :, :].rearrange("p t c -> p (t c)"), gate[:, :], ALU.mult)\
                    .then_inc(go_g.sem, 1)

            pool0 = {"fox_rows": fox_rows, "gdn_rows": gdn_rows, "decays": strict_decays, "fox_recip": fox_probs,
                     "gdn_rms": gdn_rms}

            def mix0(i):
                for s in range(L0_SLICES):
                    run_steps(MIX0[s], pool0, i)

            pool.wait_ge(row_out.sem, 16)
            pool.wait_ge(spilled.sem, 16)
            mix0(0)
            with pool.Fori(1, GDN_HEADS) as i:
                mix0(i)
            gdn_rms(GDN_HEADS - 1)
            sum_squares(1)
            sum_squares(2)

            def hg_level(i, l):
                h = 1 << l
                bb = hf[:, :].rearrange("p (c t) -> p c t", t=2 * h)
                e = he[l % 2][:, :].rearrange("p (c t) -> p c t", t=2 * h)
                ref = bb[:, :, h - 1:h].to_broadcast([P, T // (2 * h), h])
                if l >= 2:
                    pool.wait_ge(*hl_x(i, 2 * l - 2))
                pool.tensor_tensor(e[:, :, 0:h], ref, bb[:, :, 0:h], ALU.subtract).then_inc(hl_d.sem, 1)
                pool.tensor_tensor(e[:, :, h:], bb[:, :, h:], ref, ALU.subtract).then_inc(hl_d.sem, 1)

            def gated(i):
                pool.wait_ge(*hn_t(i))
                pool.wait_ge(*hgk_s(i))
                if not (isinstance(i, int) and i == 0):
                    pool.wait_ge(*hn_lo(i - 1))
                pool.tensor_tensor(hgo[:, :], hx[0][:, :], gain_gate[:, :], ALU.mult).then_inc(hn_g.sem, 1)

            def mix1(i):
                pool.wait_ge(*hg_s(i))
                if not (isinstance(i, int) and i == 0):
                    pool.wait_ge(*hn_g(i - 1))
                pool.tensor_tensor(gain_gate[:, :], hg[:, :], pp("hg_o").to_broadcast([P, T]), ALU.mult)\
                    .then_inc(hgk_s.sem, 1)
                pool.wait_ge(*hb_s(i))
                for l in range(LEVELS):
                    hg_level(i, l)

            mix1(0)
            gated(0)
            with pool.Fori(1, HG_HEADS) as i:
                mix1(i)
                gated(i)
            sum_squares(3)


def pack_params(a):
    out = np.zeros((P, PARAM_W), np.float32)

    def put(name, v):
        at, w = _p[name]
        out[:v.shape[0], at:at + w] = v

    for n, name in enumerate(("l0_mix_norm", "l0_ffn_norm", "l1_mix_norm", "l1_ffn_norm")):
        put(f"g{n}", a[name].reshape(KB, P).T)
    put("fqn", np.concatenate([a["l0_fox_q_norm"]] * 2)[:, None])
    put("fkn", np.concatenate([a["l0_fox_k_norm"]] * 2)[:, None])
    put("gdn_o", a["l0_gdn_o_norm"][:, None])
    put("hg_o", a["l1_hgrn_o_norm"][:, None])
    put("conv", a["l0_gdn_conv"].reshape(4 * 3 * GDN_HEADS, P).T)
    put("lb0", a["hgrn_lb_logits"][0].reshape(HG_HEADS, P).T)
    put("lb1", a["hgrn_lb_logits"][1].reshape(HG_HEADS, P).T)
    at = _p["row_bias"][0]
    out[R_F:R_F + FOX_HEADS, at] = a["l0_fox_f_bias"]
    out[R_A:R_A + GDN_HEADS, at] = a["l0_gdn_dt_bias"]
    out[R_A:R_A + GDN_HEADS, _p["row_a"][0]] = a["l0_gdn_A_log"]
    out[:, _p["row_sign"][0]] = np.where(np.arange(P) < R_A, -1.0, 1.0)
    out[:, _p["eps"][0]] = EPS
    return out


def kernel(**inputs):
    import concourse.bacc as bacc
    from concourse.bass_utils import run_bass_kernel_spmd

    a = {k: np.ascontiguousarray(v) for k, v in inputs.items()}
    arrays = {n: a[n] for n in ("x", "l0_w_in", "l0_w_out", "l0_w_ff1", "l0_w_ff2", "l1_w_in", "l1_w_out",
                                "l1_w_ff1", "l1_w_ff2")}
    arrays["params"] = pack_params(a)
    arrays["consts"] = constants()
    nc = bacc.Bacc("TRN2", target_bir_lowering=False, num_devices=1)
    aps = [nc.dram_tensor(f"in_{n}", v.shape, F32, kind="ExternalInput").ap() for n, v in arrays.items()]
    out = nc.dram_tensor("y", (1, T, D), F32, kind="ExternalOutput").ap()
    build(nc, *aps, out)
    r = run_bass_kernel_spmd(nc, [{f"in_{n}": v for n, v in arrays.items()}], core_ids=[0])
    return r.results[0]["y"]
```
